# Optimizing a Trainium2 kernel written in Bass

```python
import jax, jax.numpy as jnp
from jax import lax
import numpy as np
import math

D_MODEL = 1024
BATCH = 1
SEQ = 512
DEPTH = 4

N_MIXERS = 3
EPS = 1e-6
CHUNK = 128
A_WIDTH = 2 * D_MODEL
A_GROUPS = 8
A_GROUP_DIM = A_WIDTH // A_GROUPS
HEAD_DIM = 128
B_HEADS = D_MODEL // HEAD_DIM
B_PATTERNS = ((128, 1), (512, 4), (2048, 16))
N_B_GROUPS = len(B_PATTERNS)
B_WIDTH = B_HEADS * HEAD_DIM
B_IN_WIDTH = 3 * N_B_GROUPS * B_WIDTH + B_WIDTH
ROPE_DIM = HEAD_DIM // 4
ROPE_THETA = 500000.0
POOL_SIZES = (2, 4, 8, 16)
N_POOL = len(POOL_SIZES)
C_WIDTH = 2 * D_MODEL
C_GROUP = C_WIDTH // N_POOL
N_A = (DEPTH + 2) // 3
N_B = (DEPTH + 1) // 3
N_C = DEPTH // 3


def rms_norm(x, g):
    xf = x.astype(jnp.float32)
    y = xf * lax.rsqrt(jnp.mean(xf * xf, axis=-1, keepdims=True) + EPS)
    return (y * g.astype(jnp.float32)).astype(x.dtype)

def rotary_tables(seq_len):
    half = ROPE_DIM // 2
    inv_freq = jnp.power(jnp.float32(ROPE_THETA), -jnp.arange(half, dtype=jnp.float32) / half)
    ang = jnp.arange(seq_len, dtype=jnp.float32)[:, None] * inv_freq[None, :]
    return jnp.cos(ang)[None, :, None, :], jnp.sin(ang)[None, :, None, :]

def apply_partial_rotary(x, cos, sin):
    half = ROPE_DIM // 2
    x1 = x[..., :half].astype(jnp.float32)
    x2 = x[..., half:ROPE_DIM].astype(jnp.float32)
    rot = jnp.concatenate([x1 * cos - x2 * sin, x2 * cos + x1 * sin], axis=-1)
    return jnp.concatenate([rot.astype(x.dtype), x[..., ROPE_DIM:]], axis=-1)

def dilated_window_attention(q, k, v, span, dilation):
    bsz, S, H, hd = q.shape
    blk = span
    L = S // dilation
    nb = -(-L // blk)
    Lp = nb * blk

    def to_blocks(t):
        t = t.reshape(bsz, L, dilation, H, hd).transpose(0, 2, 1, 3, 4)
        t = jnp.pad(t, ((0, 0), (0, 0), (0, Lp - L), (0, 0), (0, 0)))
        return t.reshape(bsz, dilation, nb, blk, H, hd)

    def with_prev(t):
        prev = jnp.pad(t, ((0, 0), (0, 0), (1, 0), (0, 0), (0, 0), (0, 0)))[:, :, :-1]
        return jnp.concatenate([prev, t], axis=3)

    qb = to_blocks(q).astype(jnp.float32)
    kk = with_prev(to_blocks(k)).astype(jnp.float32)
    vv = with_prev(to_blocks(v)).astype(jnp.float32)
    scores = jnp.einsum('brnqhd,brnkhd->brnhqk', qb, kk) * (1.0 / np.sqrt(hd)).astype(np.float32)
    qi = jnp.arange(blk)[:, None]
    ki = jnp.arange(2 * blk)[None, :]
    dist = blk + qi - ki
    band = (dist >= 0) & (dist <= span)
    has_prev = (jnp.arange(nb) > 0)[:, None, None] | (ki >= blk)[None]
    mask = band[None] & has_prev
    scores = jnp.where(mask[None, None, :, None], scores, -jnp.inf)
    lse = jax.nn.logsumexp(scores, axis=-1)
    p = jnp.exp(scores - lse[..., None])
    o = jnp.einsum('brnhqk,brnkhd->brnqhd', p, vv)
    o = o.reshape(bsz, dilation, Lp, H, hd)[:, :, :L].transpose(0, 2, 1, 3, 4).reshape(bsz, S, H, hd)
    lse = lse.transpose(0, 1, 2, 4, 3).reshape(bsz, dilation, Lp, H)[:, :, :L]
    lse = lse.transpose(0, 2, 1, 3).reshape(bsz, S, H)
    return o, lse

def mixer_a(h, w_in, v_gain, w_s, b_s, w_out):
    bsz, S, _ = h.shape
    proj = h @ w_in
    u = proj[..., :A_WIDTH]
    v = rms_norm(proj[..., A_WIDTH:2 * A_WIDTH], v_gain)
    z = proj[..., 2 * A_WIDTH:]
    nc = S // CHUNK
    v = v.reshape(bsz, nc, CHUNK, A_GROUPS, A_GROUP_DIM)
    causal = jnp.tril(jnp.ones((CHUNK, CHUNK), dtype=bool))
    ws = jnp.where(causal[None], w_s, jnp.zeros_like(w_s))
    mixed = jnp.einsum('gij,bcjgd->bcigd', ws, v) + b_s.T[None, None, :, :, None]
    mixed = mixed.reshape(bsz, S, A_WIDTH)
    y = u * mixed * jax.nn.silu(z)
    return y @ w_out

def mixer_b(h, w_in, q_gain, k_gain, w_out):
    bsz, S, _ = h.shape
    proj = h @ w_in
    n_qkv = 3 * N_B_GROUPS * B_WIDTH
    qkv = proj[..., :n_qkv].reshape(bsz, S, 3, N_B_GROUPS, B_HEADS, HEAD_DIM)
    z = proj[..., n_qkv:]
    cos, sin = rotary_tables(S)
    outs, lses = [], []
    for g, (window, dilation) in enumerate(B_PATTERNS):
        q = apply_partial_rotary(rms_norm(qkv[:, :, 0, g], q_gain[g]), cos, sin)
        k = apply_partial_rotary(rms_norm(qkv[:, :, 1, g], k_gain[g]), cos, sin)
        o, lse = dilated_window_attention(q, k, qkv[:, :, 2, g], window // dilation, dilation)
        outs.append(o)
        lses.append(lse)
    wgt = jax.nn.softmax(jnp.stack(lses), axis=0)
    o = jnp.einsum('gbsh,gbshd->bshd', wgt, jnp.stack(outs))
    y = o.reshape(bsz, S, B_WIDTH).astype(h.dtype) * jax.nn.silu(z)
    return y @ w_out

def causal_mean(x, window):
    S = x.shape[1]
    c = jnp.cumsum(x.astype(jnp.float32), axis=1)
    c_prev = jnp.pad(c, ((0, 0), (window, 0), (0, 0)))[:, :S]
    cnt = jnp.minimum(jnp.arange(S) + 1, window).astype(jnp.float32)
    return ((c - c_prev) / cnt[None, :, None]).astype(x.dtype)

def mixer_c(h, w_in, w_grp, scale, w_out):
    bsz, S, _ = h.shape
    proj = h @ w_in
    xc = proj[..., :C_WIDTH].reshape(bsz, S, N_POOL, C_GROUP)
    z = proj[..., C_WIDTH:]
    pooled = jnp.stack([causal_mean(xc[:, :, g], w) for g, w in enumerate(POOL_SIZES)], axis=2)
    mixed = jnp.einsum('bsgc,gcd->bsgd', pooled - xc, w_grp).reshape(bsz, S, C_WIDTH) * scale
    y = mixed * jax.nn.silu(z)
    return y @ w_out

def first_inputs(seed: int = 0) -> dict:
    key = jax.random.key(seed)
    ks = jax.random.split(key, 16)
    f32 = jnp.float32

    def nrm(k, shape, fan_in):
        return jax.random.normal(k, shape, f32) * (fan_in ** -0.5)

    def gain(k, shape):
        return 1.0 + 0.1 * jax.random.normal(k, shape, f32)

    return {
        "x": jax.random.normal(ks[0], (BATCH, SEQ, D_MODEL), f32),
        "norm_gain": gain(ks[1], (DEPTH, D_MODEL)),
        "a_w_in": nrm(ks[2], (N_A, D_MODEL, 3 * A_WIDTH), D_MODEL),
        "a_v_gain": gain(ks[3], (N_A, A_WIDTH)),
        "a_w_s": nrm(ks[4], (N_A, A_GROUPS, CHUNK, CHUNK), CHUNK),
        "a_b_s": gain(ks[5], (N_A, A_GROUPS, CHUNK)),
        "a_w_out": nrm(ks[6], (N_A, A_WIDTH, D_MODEL), A_WIDTH),
        "b_w_in": nrm(ks[7], (N_B, D_MODEL, B_IN_WIDTH), D_MODEL),
        "b_q_gain": gain(ks[8], (N_B, N_B_GROUPS, HEAD_DIM)),
        "b_k_gain": gain(ks[9], (N_B, N_B_GROUPS, HEAD_DIM)),
        "b_w_out": nrm(ks[10], (N_B, B_WIDTH, D_MODEL), B_WIDTH),
        "c_w_in": nrm(ks[11], (N_C, D_MODEL, 2 * C_WIDTH), D_MODEL),
        "c_w_grp": nrm(ks[12], (N_C, N_POOL, C_GROUP, C_GROUP), C_GROUP),
        "c_scale": gain(ks[13], (N_C, C_WIDTH)),
        "c_w_out": nrm(ks[14], (N_C, C_WIDTH, D_MODEL), C_WIDTH),
    }

def first_block(x, norm_gain, a_w_in, a_v_gain, a_w_s, a_b_s, a_w_out,
              b_w_in, b_q_gain, b_k_gain, b_w_out,
              c_w_in, c_w_grp, c_scale, c_w_out):
    for i in range(DEPTH):
        kind, j = i % N_MIXERS, i // N_MIXERS
        h = rms_norm(x, norm_gain[i])
        if kind == 0:
            y = mixer_a(h, a_w_in[j], a_v_gain[j], a_w_s[j], a_b_s[j], a_w_out[j])
        elif kind == 1:
            y = mixer_b(h, b_w_in[j], b_q_gain[j], b_k_gain[j], b_w_out[j])
        else:
            y = mixer_c(h, c_w_in[j], c_w_grp[j], c_scale[j], c_w_out[j])
        x = x + y.astype(x.dtype)
    return x


DEPTH_2 = 2

CHUNK_2 = 64
Q_BLOCK = 128
RMS_EPS = 1e-6
LN_EPS = 1e-5
ROPE_FRACTION = 4
DIFF_HEADS = D_MODEL // 256
DIFF_HEAD_DIM = 64
DIFF_WIDTH = DIFF_HEADS * 2 * DIFF_HEAD_DIM
CONV_CHANNELS = D_MODEL - DIFF_WIDTH
CONV_WIDTH = 31
SSM_CHANNELS = D_MODEL // 4
SSM_GROUP = 16
SSM_GROUPS = SSM_CHANNELS // SSM_GROUP
SSM_STATE = 64
DT_MIN = 1e-3
DT_MAX = 1e-1
MLA_V_DIM = 128
MLA_HEADS = (D_MODEL - SSM_CHANNELS) // MLA_V_DIM
MLA_NOPE_DIM = 128
MLA_ROPE_DIM = 64
MLA_Q_RANK = D_MODEL // 4
MLA_KV_RANK = D_MODEL // 8
MLA_ROPE_THETA = 10000.0
D_FF = -(-8 * D_MODEL // (3 * 256)) * 256
EVEN_IN = 3 * DIFF_WIDTH + 2 * CONV_CHANNELS
ODD_IN = SSM_CHANNELS + MLA_Q_RANK + MLA_KV_RANK + MLA_ROPE_DIM


def rmsnorm(x, g):
    x32 = x.astype(jnp.float32)
    y = x32 * lax.rsqrt(jnp.mean(x32 * x32, axis=-1, keepdims=True) + RMS_EPS)
    return (y * g.astype(jnp.float32)).astype(x.dtype)

def layernorm(x, g, b):
    x32 = x.astype(jnp.float32)
    mu = jnp.mean(x32, axis=-1, keepdims=True)
    xc = x32 - mu
    y = xc * lax.rsqrt(jnp.mean(xc * xc, axis=-1, keepdims=True) + LN_EPS)
    return (y * g.astype(jnp.float32) + b.astype(jnp.float32)).astype(x.dtype)

def rope_tables(s, rot_dim, theta):
    inv = theta ** (-jnp.arange(0, rot_dim, 2, dtype=jnp.float32) / rot_dim)
    ang = jnp.arange(s, dtype=jnp.float32)[:, None] * inv[None, :]
    return jnp.cos(ang), jnp.sin(ang)

def apply_rope(x, cos, sin):
    half = cos.shape[-1]
    shape = (1, cos.shape[0]) + (1,) * (x.ndim - 3) + (half,)
    c = cos.reshape(shape).astype(x.dtype)
    s = sin.reshape(shape).astype(x.dtype)
    x1 = x[..., :half]
    x2 = x[..., half:2 * half]
    return jnp.concatenate([x1 * c - x2 * s, x2 * c + x1 * s, x[..., 2 * half:]], axis=-1)

def chunk_causal_mask(i, s):
    qpos = i * Q_BLOCK + jnp.arange(Q_BLOCK)
    kpos = jnp.arange(s)
    return (kpos // CHUNK_2)[None, :] <= (qpos // CHUNK_2)[:, None]

def sweep_query_blocks(block_fn, q):
    b, s = q.shape[:2]
    nb = s // Q_BLOCK
    qb = jnp.moveaxis(q.reshape((b, nb, Q_BLOCK) + q.shape[2:]), 1, 0)
    out = lax.map(lambda a: block_fn(a[0], a[1]), (jnp.arange(nb), qb))
    out = jnp.moveaxis(out, 0, 1)
    return out.reshape((b, s) + out.shape[3:])

def sandwich(x, g_pre, g_post, fn):
    return x + rmsnorm(fn(rmsnorm(x, g_pre)), g_post)

def swiglu(h, w_gate, w_up, w_down):
    return (jax.nn.silu(h @ w_gate) * (h @ w_up)) @ w_down

def diff_attention(qkv, layer_idx, lq1, lk1, lq2, lk2, subln, cos, sin):
    b, s, _ = qkv.shape
    f32 = jnp.float32
    q = qkv[..., :DIFF_WIDTH].reshape(b, s, DIFF_HEADS, 2, DIFF_HEAD_DIM)
    k = qkv[..., DIFF_WIDTH:2 * DIFF_WIDTH].reshape(b, s, DIFF_HEADS, 2, DIFF_HEAD_DIM)
    v = qkv[..., 2 * DIFF_WIDTH:].reshape(b, s, DIFF_HEADS, 2 * DIFF_HEAD_DIM)
    q = apply_rope(q, cos, sin)
    k = apply_rope(k, cos, sin)
    lam_init = 0.8 - 0.6 * math.exp(-0.3 * layer_idx)
    lam = (jnp.exp(jnp.sum(lq1.astype(f32) * lk1.astype(f32)))
           - jnp.exp(jnp.sum(lq2.astype(f32) * lk2.astype(f32))) + lam_init)
    scale = DIFF_HEAD_DIM ** -0.5

    def block(i, qb):
        sc = jnp.einsum('bqhcd,bkhcd->bhcqk', qb, k, preferred_element_type=f32) * scale
        p = jax.nn.softmax(jnp.where(chunk_causal_mask(i, s), sc, -jnp.inf), axis=-1)
        w = p[:, :, 0] - lam * p[:, :, 1]
        return jnp.einsum('bhqk,bkhe->bqhe', w.astype(v.dtype), v)

    o = sweep_query_blocks(block, q)
    o = rmsnorm(o, subln) * (1.0 - lam_init)
    return o.reshape(b, s, DIFF_WIDTH)

def conformer_conv(g, dw_w, dw_b, ln_g, ln_b):
    u = g[..., :CONV_CHANNELS] * jax.nn.sigmoid(g[..., CONV_CHANNELS:])
    y = lax.conv_general_dilated(
        u, dw_w[:, None, :].astype(u.dtype), window_strides=(1,),
        padding=[(CONV_WIDTH - 1, 0)], dimension_numbers=('NWC', 'WIO', 'NWC'),
        feature_group_count=CONV_CHANNELS) + dw_b
    return jax.nn.silu(layernorm(y, ln_g, ln_b))

def s5_ssm(u, a_re, a_im, log_dt, b_re, b_im, c_re, c_im, d_skip, w_glu, b_glu):
    b, s, _ = u.shape
    f32 = jnp.float32
    ug = u.reshape(b, s, SSM_GROUPS, SSM_GROUP).astype(f32)
    lr = a_re.astype(f32)
    li = a_im.astype(f32)
    dt = jnp.exp(log_dt.astype(f32))[:, None]
    mag = jnp.exp(lr * dt)
    ab_re = mag * jnp.cos(li * dt)
    ab_im = mag * jnp.sin(li * dt)
    den = lr * lr + li * li
    n_re = ab_re - 1.0
    f_re = (n_re * lr + ab_im * li) / den
    f_im = (ab_im * lr - n_re * li) / den
    br = b_re.astype(f32)
    bi = b_im.astype(f32)
    bb_re = f_re[:, :, None] * br - f_im[:, :, None] * bi
    bb_im = f_re[:, :, None] * bi + f_im[:, :, None] * br
    bu_re = jnp.einsum('bsgh,gph->bsgp', ug, bb_re)
    bu_im = jnp.einsum('bsgh,gph->bsgp', ug, bb_im)
    aa_re = jnp.broadcast_to(ab_re, bu_re.shape)
    aa_im = jnp.broadcast_to(ab_im, bu_im.shape)

    def combine(e1, e2):
        ar1, ai1, xr1, xi1 = e1
        ar2, ai2, xr2, xi2 = e2
        return (ar2 * ar1 - ai2 * ai1, ar2 * ai1 + ai2 * ar1,
                ar2 * xr1 - ai2 * xi1 + xr2, ar2 * xi1 + ai2 * xr1 + xi2)

    _, _, x_re, x_im = lax.associative_scan(combine, (aa_re, aa_im, bu_re, bu_im), axis=1)
    y = (jnp.einsum('bsgp,ghp->bsgh', x_re, c_re.astype(f32))
         - jnp.einsum('bsgp,ghp->bsgh', x_im, c_im.astype(f32))
         + d_skip.astype(f32)[None, None] * ug)
    y = y.reshape(b, s, SSM_CHANNELS).astype(u.dtype)
    z = jax.nn.gelu(y)
    return z * jax.nn.sigmoid(z @ w_glu + b_glu)

def mla_attention(c_q, c_kv, k_r, q_norm, w_uq, kv_norm, w_ukv, cos, sin):
    b, s, _ = c_q.shape
    f32 = jnp.float32
    q = (rmsnorm(c_q, q_norm) @ w_uq).reshape(b, s, MLA_HEADS, MLA_NOPE_DIM + MLA_ROPE_DIM)
    q = jnp.concatenate([q[..., :MLA_NOPE_DIM], apply_rope(q[..., MLA_NOPE_DIM:], cos, sin)], axis=-1)
    kv = (rmsnorm(c_kv, kv_norm) @ w_ukv).reshape(b, s, MLA_HEADS, MLA_NOPE_DIM + MLA_V_DIM)
    k_rope = jnp.broadcast_to(apply_rope(k_r, cos, sin)[:, :, None, :], (b, s, MLA_HEADS, MLA_ROPE_DIM))
    k = jnp.concatenate([kv[..., :MLA_NOPE_DIM], k_rope], axis=-1)
    v = kv[..., MLA_NOPE_DIM:]
    scale = (MLA_NOPE_DIM + MLA_ROPE_DIM) ** -0.5

    def block(i, qb):
        sc = jnp.einsum('bqhd,bkhd->bhqk', qb, k, preferred_element_type=f32) * scale
        p = jax.nn.softmax(jnp.where(chunk_causal_mask(i, s), sc, -jnp.inf), axis=-1)
        return jnp.einsum('bhqk,bkhd->bqhd', p.astype(v.dtype), v)

    o = sweep_query_blocks(block, q)
    return o.reshape(b, s, MLA_HEADS * MLA_V_DIM)

def even_mixer(t, layer_idx, w_in, lq1, lk1, lq2, lk2, subln, dw_w, dw_b, ln_g, ln_b, w_out, cos, sin):
    proj = t @ w_in
    y_a = diff_attention(proj[..., :3 * DIFF_WIDTH], layer_idx, lq1, lk1, lq2, lk2, subln, cos, sin)
    y_b = conformer_conv(proj[..., 3 * DIFF_WIDTH:], dw_w, dw_b, ln_g, ln_b)
    return jnp.concatenate([y_a, y_b], axis=-1) @ w_out

def odd_mixer(t, w_in, a_re, a_im, log_dt, b_re, b_im, c_re, c_im, d_skip, w_glu, b_glu,
              q_norm, w_uq, kv_norm, w_ukv, w_out, cos, sin):
    proj = t @ w_in
    o1 = SSM_CHANNELS
    o2 = o1 + MLA_Q_RANK
    o3 = o2 + MLA_KV_RANK
    y_c = s5_ssm(proj[..., :o1], a_re, a_im, log_dt, b_re, b_im, c_re, c_im, d_skip, w_glu, b_glu)
    y_d = mla_attention(proj[..., o1:o2], proj[..., o2:o3], proj[..., o3:], q_norm, w_uq, kv_norm, w_ukv, cos, sin)
    return jnp.concatenate([y_c, y_d], axis=-1) @ w_out

def second_inputs(seed: int = 0) -> dict:
    key = jax.random.key(seed)
    ks = iter(jax.random.split(key, 64))
    f32 = jnp.float32

    def nrm(shape, scale):
        return jax.random.normal(next(ks), shape, f32) * scale

    def gain(n):
        return 1.0 + 0.02 * jax.random.normal(next(ks), (n,), f32)

    d = D_MODEL
    inp = {}
    inp['x'] = nrm((BATCH, SEQ, d), 1.0)
    inp['l0_mix_pre'] = gain(d)
    inp['l0_mix_post'] = gain(d)
    inp['l0_w_in'] = nrm((d, EVEN_IN), d ** -0.5)
    inp['l0_lambda_q1'] = nrm((DIFF_HEAD_DIM,), 0.1)
    inp['l0_lambda_k1'] = nrm((DIFF_HEAD_DIM,), 0.1)
    inp['l0_lambda_q2'] = nrm((DIFF_HEAD_DIM,), 0.1)
    inp['l0_lambda_k2'] = nrm((DIFF_HEAD_DIM,), 0.1)
    inp['l0_subln'] = gain(2 * DIFF_HEAD_DIM)
    inp['l0_dw_w'] = nrm((CONV_WIDTH, CONV_CHANNELS), CONV_WIDTH ** -0.5)
    inp['l0_dw_b'] = nrm((CONV_CHANNELS,), 0.02)
    inp['l0_conv_ln_g'] = gain(CONV_CHANNELS)
    inp['l0_conv_ln_b'] = nrm((CONV_CHANNELS,), 0.02)
    inp['l0_w_out'] = nrm((DIFF_WIDTH + CONV_CHANNELS, d), (DIFF_WIDTH + CONV_CHANNELS) ** -0.5)
    inp['l0_ffn_pre'] = gain(d)
    inp['l0_ffn_post'] = gain(d)
    inp['l0_w_gate'] = nrm((d, D_FF), d ** -0.5)
    inp['l0_w_up'] = nrm((d, D_FF), d ** -0.5)
    inp['l0_w_down'] = nrm((D_FF, d), D_FF ** -0.5)
    inp['l1_mix_pre'] = gain(d)
    inp['l1_mix_post'] = gain(d)
    inp['l1_w_in'] = nrm((d, ODD_IN), d ** -0.5)
    inp['l1_a_re'] = -0.5 + nrm((SSM_GROUPS, SSM_STATE), 0.01)
    inp['l1_a_im'] = (jnp.pi * jnp.arange(SSM_STATE, dtype=f32))[None, :] + nrm((SSM_GROUPS, SSM_STATE), 0.01)
    inp['l1_log_dt'] = jax.random.uniform(next(ks), (SSM_GROUPS,), f32, math.log(DT_MIN), math.log(DT_MAX))
    inp['l1_b_re'] = nrm((SSM_GROUPS, SSM_STATE, SSM_GROUP), (2 * SSM_GROUP) ** -0.5)
    inp['l1_b_im'] = nrm((SSM_GROUPS, SSM_STATE, SSM_GROUP), (2 * SSM_GROUP) ** -0.5)
    inp['l1_c_re'] = nrm((SSM_GROUPS, SSM_GROUP, SSM_STATE), (2 * SSM_STATE) ** -0.5)
    inp['l1_c_im'] = nrm((SSM_GROUPS, SSM_GROUP, SSM_STATE), (2 * SSM_STATE) ** -0.5)
    inp['l1_d_skip'] = nrm((SSM_GROUPS, SSM_GROUP), 1.0)
    inp['l1_w_glu'] = nrm((SSM_CHANNELS, SSM_CHANNELS), SSM_CHANNELS ** -0.5)
    inp['l1_b_glu'] = nrm((SSM_CHANNELS,), 0.02)
    inp['l1_q_norm'] = gain(MLA_Q_RANK)
    inp['l1_w_uq'] = nrm((MLA_Q_RANK, MLA_HEADS * (MLA_NOPE_DIM + MLA_ROPE_DIM)), MLA_Q_RANK ** -0.5)
    inp['l1_kv_norm'] = gain(MLA_KV_RANK)
    inp['l1_w_ukv'] = nrm((MLA_KV_RANK, MLA_HEADS * (MLA_NOPE_DIM + MLA_V_DIM)), MLA_KV_RANK ** -0.5)
    inp['l1_w_out'] = nrm((SSM_CHANNELS + MLA_HEADS * MLA_V_DIM, d), (SSM_CHANNELS + MLA_HEADS * MLA_V_DIM) ** -0.5)
    inp['l1_ffn_pre'] = gain(d)
    inp['l1_ffn_post'] = gain(d)
    inp['l1_w_gate'] = nrm((d, D_FF), d ** -0.5)
    inp['l1_w_up'] = nrm((d, D_FF), d ** -0.5)
    inp['l1_w_down'] = nrm((D_FF, d), D_FF ** -0.5)
    return inp

def second_block(x,
              l0_mix_pre, l0_mix_post, l0_w_in, l0_lambda_q1, l0_lambda_k1, l0_lambda_q2, l0_lambda_k2,
              l0_subln, l0_dw_w, l0_dw_b, l0_conv_ln_g, l0_conv_ln_b, l0_w_out,
              l0_ffn_pre, l0_ffn_post, l0_w_gate, l0_w_up, l0_w_down,
              l1_mix_pre, l1_mix_post, l1_w_in, l1_a_re, l1_a_im, l1_log_dt, l1_b_re, l1_b_im,
              l1_c_re, l1_c_im, l1_d_skip, l1_w_glu, l1_b_glu, l1_q_norm, l1_w_uq, l1_kv_norm, l1_w_ukv,
              l1_w_out, l1_ffn_pre, l1_ffn_post, l1_w_gate, l1_w_up, l1_w_down):
    s = x.shape[1]
    cos_a, sin_a = rope_tables(s, DIFF_HEAD_DIM // ROPE_FRACTION, ROPE_THETA)
    cos_d, sin_d = rope_tables(s, MLA_ROPE_DIM, MLA_ROPE_THETA)

    def layer0(h):
        h = sandwich(h, l0_mix_pre, l0_mix_post, lambda t: even_mixer(
            t, 0, l0_w_in, l0_lambda_q1, l0_lambda_k1, l0_lambda_q2, l0_lambda_k2, l0_subln,
            l0_dw_w, l0_dw_b, l0_conv_ln_g, l0_conv_ln_b, l0_w_out, cos_a, sin_a))
        return sandwich(h, l0_ffn_pre, l0_ffn_post, lambda t: swiglu(t, l0_w_gate, l0_w_up, l0_w_down))

    def layer1(h):
        h = sandwich(h, l1_mix_pre, l1_mix_post, lambda t: odd_mixer(
            t, l1_w_in, l1_a_re, l1_a_im, l1_log_dt, l1_b_re, l1_b_im, l1_c_re, l1_c_im, l1_d_skip,
            l1_w_glu, l1_b_glu, l1_q_norm, l1_w_uq, l1_kv_norm, l1_w_ukv, l1_w_out, cos_d, sin_d))
        return sandwich(h, l1_ffn_pre, l1_ffn_post, lambda t: swiglu(t, l1_w_gate, l1_w_up, l1_w_down))

    layers = (layer0, layer1)
    h = x
    for i in range(DEPTH_2):
        h = layers[i](h)
    return h


def setup_inputs(seed=0):
    out = dict(first_inputs(seed))
    for name, value in second_inputs(seed + 1).items():
        if name != "x":
            out[name + "_2"] = value
    return out


def reference(
    x, norm_gain, a_w_in, a_v_gain, a_w_s, a_b_s, a_w_out, b_w_in, b_q_gain, b_k_gain, b_w_out,
    c_w_in, c_w_grp, c_scale, c_w_out, l0_mix_pre_2, l0_mix_post_2, l0_w_in_2, l0_lambda_q1_2,
    l0_lambda_k1_2, l0_lambda_q2_2, l0_lambda_k2_2, l0_subln_2, l0_dw_w_2, l0_dw_b_2,
    l0_conv_ln_g_2, l0_conv_ln_b_2, l0_w_out_2, l0_ffn_pre_2, l0_ffn_post_2, l0_w_gate_2,
    l0_w_up_2, l0_w_down_2, l1_mix_pre_2, l1_mix_post_2, l1_w_in_2, l1_a_re_2, l1_a_im_2,
    l1_log_dt_2, l1_b_re_2, l1_b_im_2, l1_c_re_2, l1_c_im_2, l1_d_skip_2, l1_w_glu_2,
    l1_b_glu_2, l1_q_norm_2, l1_w_uq_2, l1_kv_norm_2, l1_w_ukv_2, l1_w_out_2, l1_ffn_pre_2,
    l1_ffn_post_2, l1_w_gate_2, l1_w_up_2, l1_w_down_2,
):
    x = first_block(
        x, norm_gain, a_w_in, a_v_gain, a_w_s, a_b_s, a_w_out, b_w_in, b_q_gain, b_k_gain,
        b_w_out, c_w_in, c_w_grp, c_scale, c_w_out,
    )
    return second_block(
        x, l0_mix_pre_2, l0_mix_post_2, l0_w_in_2, l0_lambda_q1_2, l0_lambda_k1_2,
        l0_lambda_q2_2, l0_lambda_k2_2, l0_subln_2, l0_dw_w_2, l0_dw_b_2, l0_conv_ln_g_2,
        l0_conv_ln_b_2, l0_w_out_2, l0_ffn_pre_2, l0_ffn_post_2, l0_w_gate_2, l0_w_up_2,
        l0_w_down_2, l1_mix_pre_2, l1_mix_post_2, l1_w_in_2, l1_a_re_2, l1_a_im_2, l1_log_dt_2,
        l1_b_re_2, l1_b_im_2, l1_c_re_2, l1_c_im_2, l1_d_skip_2, l1_w_glu_2, l1_b_glu_2,
        l1_q_norm_2, l1_w_uq_2, l1_kv_norm_2, l1_w_ukv_2, l1_w_out_2, l1_ffn_pre_2,
        l1_ffn_post_2, l1_w_gate_2, l1_w_up_2, l1_w_down_2,
    )


_drawn_inputs = setup_inputs


def setup_inputs(seed=0):
    import zlib

    import numpy as np

    out = dict(_drawn_inputs(seed))
    spreads = {}
    factors = {'b_q_gain': 4.858,
     'b_k_gain': 4.257,
     'l0_mix_post_2': 4.047,
     'l0_lambda_q1_2': 8.0,
     'l0_subln_2': 4.998,
     'l0_conv_ln_g_2': 5.233,
     'l0_conv_ln_b_2': 4.889,
     'l0_ffn_pre_2': 3.865,
     'l0_ffn_post_2': 5.583,
     'l1_mix_pre_2': 4.817,
     'l1_mix_post_2': 22.075,
     'l1_a_re_2': 64.0,
     'l1_a_im_2': 22.632,
     'l1_log_dt_2': 25.36,
     'l1_b_re_2': 29.488,
     'l1_b_im_2': 34.072,
     'l1_c_re_2': 29.472,
     'l1_c_im_2': 32.184,
     'l1_b_glu_2': 64.0,
     'l1_q_norm_2': 8.0,
     'l1_kv_norm_2': 6.965,
     'l1_ffn_pre_2': 14.516,
     'l1_ffn_post_2': 31.478}
    for name, (base, spread) in spreads.items():
        noise = np.random.default_rng([zlib.crc32(name.encode()), seed]).standard_normal(out[name].shape)
        drawn = base * np.exp(spread * noise) if base else spread * noise
        out[name] = __import__('jax').numpy.asarray(drawn.astype(out[name].dtype))
    for name, factor in factors.items():
        out[name] = (out[name] * factor).astype(out[name].dtype)
    return out
```

```python
import math
from contextlib import ExitStack

import numpy as np

import concourse.bass as bass
from concourse import mybir
from concourse.alu_op_type import AluOpType as ALU

ACT = mybir.ActivationFunctionType
AXIS = mybir.AxisListType
F32 = mybir.dt.float32
F32R = mybir.dt.float32r
I32 = mybir.dt.int32

P = 128
T = 512
D = 1024
KD = D // P
NBLK = T // P
RAW_SLOTS = 2
SLOTS = 4
AHEAD = 3
UNIT = 1024
CLASSES = 4

A_WIDTH, A_GROUPS = 2048, 8
A_TILES = A_WIDTH // P
B_HEADS, B_PATTERNS = 8, 3
C_POOLS, C_GROUP_TILES = 4, 4
POOL_SIZES = (2, 4, 8, 16)
D_FF = 2816
FF_GROUPS = (8, 8, 6)
assert sum(FF_GROUPS) * P == D_FF
DIFF_HEADS, DIFF_DIM = 4, 64
CONV_TILES, CONV_WIDTH = 4, 31
SSM_TILES = 8
MLA_HEADS = 6
EPS, LN_EPS = 1e-6, 1e-5
LAM_INIT = 0.2

A_UNITS = 16 + 2 * (16 + 8)
B_UNITS = 2 * (4 * B_PATTERNS + 4 * 2 * B_PATTERNS + 4) + 8
C_UNITS = 2 * (20 + 8)
E_UNITS = 20 + 8
FF_UNITS = 2 * sum(FF_GROUPS) + 8 * len(FF_GROUPS)
O_UNITS = 12 + 8
STAGES = (("a0", A_UNITS), ("b", B_UNITS), ("c", C_UNITS), ("a1", A_UNITS), ("e", E_UNITS), ("f0", FF_UNITS),
          ("o", O_UNITS), ("f1", FF_UNITS))
FIRST = {}
TOTAL = 0
for _name, _n in STAGES:
    FIRST[_name] = TOTAL
    TOTAL += _n
assert TOTAL % SLOTS == 0 and all(n % SLOTS == 0 for n in FIRST.values())

COLUMNS = {}
_at = 0
for _name, _n in (("norm", 4 * 8), ("e_pre", 8), ("e_post", 8), ("f0_pre", 8), ("f0_post", 8), ("o_pre", 8),
                  ("o_post", 8), ("f1_pre", 8), ("f1_post", 8), ("a_v", 2 * 16), ("b_q", 3), ("b_k", 3),
                  ("c_scale", 16), ("subln", 1), ("dw_w", 4 * 31), ("dw_b", 4), ("ln_g", 4), ("ln_b", 4),
                  ("glu_b", 2), ("q_norm", 2), ("kv_norm", 1), ("a_re", 8), ("a_im", 8), ("log_dt", 8),
                  ("d_skip", 2), ("lambda", 4 * 64)):
    COLUMNS[_name] = _at
    _at += _n
N_COLUMNS = _at

CONST = {}
_at = 0
for _name, _n in (("ident", 128), ("ones", 128), ("causal", 128), ("chunk", 512), ("rot_b", 128), ("rot_e", 128),
                  ("rot_o", 128), ("inv_count", 4 * 16), ("eps", 1), ("ln_eps", 1)):
    CONST[_name] = _at
    _at += _n
N_CONST = _at
MASKED = -1.0e30


class Unit:

    def __init__(self, first, loop=None, per=0):
        assert per % SLOTS == 0
        self.first, self.loop, self.per = first, loop, per
        self.slot, self.raw = first % SLOTS, first % RAW_SLOTS

    def __add__(self, n):
        return Unit(self.first + n, self.loop, self.per)

    def count(self, n):
        return self.first + n if self.loop is None else self.loop * self.per + (self.first + n)

    def loads(self):
        v = 16 * (self.first // RAW_SLOTS + 1)
        return v if self.loop is None else self.loop * (16 * self.per // RAW_SLOTS) + v


def lin(base, loop, per):
    return base if loop is None else loop * per + base

NAMES = [n for n, _ in STAGES]
SANDWICHED = [n for n in NAMES if n in ("e", "f0", "o", "f1")]
H_NO = {n: i for i, n in enumerate(NAMES)}
P_NO = {n: i for i, n in enumerate(SANDWICHED)}
R_PRE, R_POST, Q_NO = {}, {}, {}
for _i, _n in enumerate(NAMES):
    R_PRE[_n] = len(R_PRE) + len(R_POST)
    if _i == 0 or NAMES[_i - 1] not in SANDWICHED:
        Q_NO[R_PRE[_n]] = len(Q_NO)
    if _n in SANDWICHED:
        R_POST[_n] = len(R_PRE) + len(R_POST)
        Q_NO[R_POST[_n]] = len(Q_NO)
OUTS = {"a0": 2, "b": 1, "c": 4, "a1": 2, "e": 1, "f0": 3, "o": 1, "f1": 3}
Y_TILES = {"a0": 16, "b": 8, "c": 16, "a1": 16, "e": 8, "f0": 22, "o": 8, "f1": 22}
O_NO = {n: sum(OUTS[q] for q in NAMES[:i]) for i, n in enumerate(NAMES)}
Y_BASE = {n: sum(Y_TILES[q] for q in NAMES[:i]) for i, n in enumerate(NAMES)}
TABLE_OF = {"a0": 0, "b": 1, "a1": 2, "e": 3, "o": 4}
TABLED = [n for n in NAMES if n in TABLE_OF]
AGAIN = {n: sum(q[0] == n[0] for q in NAMES[:i]) for i, n in enumerate(NAMES)}


def build(nc, stream, x_in, params_in, const_in, tables_in, ssm_in, x_out):
    names, total = NAMES, TOTAL
    ctx = ExitStack()

    def sb(name, shape, dtype=F32):
        return ctx.enter_context(nc.sbuf_tensor(name, shape, dtype))

    def sem(name):
        return ctx.enter_context(nc.semaphore(name))

    with ctx:
        x = sb("x", [P, KD, T])
        h_high = sb("h_high", [P, KD, T], F32R)
        h_low = sb("h_low", [P, KD, T], F32R)
        y_high = sb("y_high", [P, KD, T], F32R)
        y_low = sb("y_low", [P, KD, T], F32R)
        raw = sb("raw", [P, RAW_SLOTS, UNIT])
        w_high = sb("w_high", [P, SLOTS, UNIT], F32R)
        w_low = sb("w_low", [P, SLOTS, UNIT], F32R)
        params = sb("params", [P, N_COLUMNS])
        const = sb("const", [P, N_CONST])
        table = sb("table", [P, 2176])
        root = sb("root", [P, T])
        rstd = sb("rstd", [P, T])
        full = sb("full", [P, 2, T])
        sq = sb("sq", [P, T])
        ssq = sb("ssq", [P, T])
        arena = sb("arena", [P, 12800])
        work = sb("work", [P, 2304])
        small = sb("small", [P, 168])
        norm_col = sb("norm_col", [P, 16])
        norm_sums, norm_roots, norm_rstds = (norm_col[:, 4 * n:4 * n + 4] for n in range(3))
        norm_spare, norm_zero = norm_col[:, 12:13], norm_col[:, 13:14]
        ps = ctx.enter_context(nc.psum_tensor("ps", [P, 8, T], F32))

        def view(at, *shape):
            n = int(np.prod(shape))
            assert at + n <= 12800, (at, n)
            a = arena[:, at:at + n]
            if len(shape) == 1:
                return a
            letters = "abcd"[:len(shape)]
            sizes = {c: s for c, s in zip(letters[1:], shape[1:])}
            return a.rearrange(f"p ({' '.join(letters)}) -> p {' '.join(letters)}", **sizes)

        def par(name, i=0, n=1):
            return params[:, COLUMNS[name] + i:COLUMNS[name] + i + n]

        def con(name, i=0, n=1):
            return const[:, CONST[name] + i:CONST[name] + i + n]

        ident, ones = con("ident", 0, P), con("ones", 0, P)

        x_loaded, params_loaded, const_loaded = [sem(f"x_loaded_{k}") for k in range(KD)], sem("params_loaded"), sem("const_loaded")
        table_loaded, x_stored = sem("table_loaded"), sem("x_stored")
        weights_loaded = [sem(f"weights_loaded_{s}") for s in range(RAW_SLOTS)]
        weights_high, weights_low, units_done = sem("weights_high"), sem("weights_low"), sem("units_done")
        norm_gathered = sem("norm_gathered")
        norm_squared, norm_summed, norm_added = sem("norm_squared"), sem("norm_summed"), sem("norm_added")
        root_done, rstd_done, rstd_spread = sem("root_done"), sem("rstd_done"), sem("rstd_spread")
        h_full, h_high_done, h_low_done = sem("h_full"), sem("h_high_done"), sem("h_low_done")
        y_high_done, y_low_done = sem("y_high_done"), sem("y_low_done")
        out_free = sem("out_free")
        a_masked = sem("a_masked")
        post_scaled, post_summed = sem("post_scaled"), sem("post_summed")
        post_even, post_odd = sem("post_even"), sem("post_odd")
        c_pool, c_diff_high, c_diff_low = sem("c_pool"), sem("c_diff_high"), sem("c_diff_low")
        c_silu, c_gated = sem("c_silu"), sem("c_gated")
        f_silu, f_full = sem("f_silu"), sem("f_full")
        b_v_copied, b_squared, b_gained, b_ss = sem("b_v_copied"), sem("b_squared"), sem("b_gained"), sem("b_ss")
        b_rot, b_turned, b_cosed, b_qk_done = sem("b_rot"), sem("b_turned"), sem("b_cosed"), sem("b_qk_done")
        b_root_done, b_rk_done, b_rq_done = sem("b_root_done"), sem("b_rk_done"), sem("b_rq_done")
        b_spread, b_k_done = sem("b_spread"), sem("b_k_done")
        b_scores, b_soft, b_exp = sem("b_scores"), sem("b_soft"), sem("b_exp")
        b_t_few, b_t_done, b_pt_copied, b_pv = sem("b_t_few"), sem("b_t_done"), sem("b_pt_copied"), sem("b_pv")
        b_o_copied, b_silu, b_gated = sem("b_o_copied"), sem("b_silu"), sem("b_gated")
        e_padded, e_lam_done, e_lam_exp = sem("e_padded"), sem("e_lam_done"), sem("e_lam_exp")
        e_sig, e_gated, e_tap, e_tapped, e_added = sem("e_sig"), sem("e_gated"), sem("e_tap"), sem("e_tapped"), sem("e_added")
        e_v_copied, e_raw, e_rot, e_turned = sem("e_v_copied"), sem("e_raw"), sem("e_rot"), sem("e_turned")
        e_cosed, e_qk_done, e_scores, e_soft, e_exp = sem("e_cosed"), sem("e_qk_done"), sem("e_scores"), sem("e_soft"), sem("e_exp")
        e_t_done, e_wt_copied, e_pv, e_o_copied = sem("e_t_done"), sem("e_wt_copied"), sem("e_pv"), sem("e_o_copied")
        e_sub_sum, e_sub_root, e_sub_rstd, e_y_full = sem("e_sub_sum"), sem("e_sub_root"), sem("e_sub_rstd"), sem("e_y_full")
        e_ln_mean, e_centred, e_ln_squared = sem("e_ln_mean"), sem("e_centred"), sem("e_ln_squared")
        e_ln_sum, e_ln_root, e_ln_scaled = sem("e_ln_sum"), sem("e_ln_root"), sem("e_ln_scaled")
        e_ln_rstd, e_ln_spread, e_mix = sem("e_ln_rstd"), sem("e_ln_spread"), sem("e_mix")
        e_joined, zero_done = sem("e_joined"), sem("zero_done")
        e_sub_arg, e_sub_spread = sem("e_sub_arg"), sem("e_sub_spread")
        ssm_loaded, o_prep, o_prepared = sem("ssm_loaded"), sem("o_prep"), sem("o_prepared")
        o_spread, o_scaled, o_inverse = sem("o_spread"), sem("o_scaled"), sem("o_inverse")
        o_c_done, o_small_done = sem("o_c_done"), sem("o_small_done")
        o_e_done, o_lin, o_squared, o_sums, o_roots = sem("o_e_done"), sem("o_lin"), sem("o_squared"), sem("o_sums"), sem("o_roots")
        o_rstds, o_normed, o_n_high, o_n_low = sem("o_rstds"), sem("o_normed"), sem("o_n_high"), sem("o_n_low")
        o_rot, o_turned, o_cosed, o_roped = sem("o_rot"), sem("o_turned"), sem("o_cosed"), sem("o_roped")
        o_bu, o_ssm, o_cy, o_taken, o_gelu = sem("o_bu"), sem("o_ssm"), sem("o_cy"), sem("o_taken"), sem("o_gelu")
        o_z_high, o_z_low, o_sig, o_gated, o_small = sem("o_z_high"), sem("o_z_low"), sem("o_sig"), sem("o_gated"), sem("o_small")
        o_scores, o_soft, o_exp = sem("o_scores"), sem("o_soft"), sem("o_exp")
        o_t_done, o_wt_copied, o_pv = sem("o_t_done"), sem("o_wt_copied"), sem("o_pv")
        v_copied, v_squared, v_stats, v_root = sem("v_copied"), sem("v_squared"), sem("v_stats"), sem("v_root")
        a_vector, a_silu, mix_done = sem("a_vector"), sem("a_silu"), sem("mix_done")
        v_stats_r = sem("v_rstd")

        def split_high(act, u):
            if u.loop is None and u.first >= total:
                return
            act.wait_ge(weights_loaded[u.raw], u.loads())
            if u.first >= SLOTS:
                act.wait_ge(units_done, u.count(1 - SLOTS))
            nc.scalar.activation(w_high[:, u.slot], raw[:, u.raw], ACT.Copy).then_inc(weights_high, 1)

        def split_low(dve, u):
            if u.loop is None and u.first >= total:
                return
            dve.wait_ge(weights_high, u.count(1))
            nc.vector.tensor_tensor(w_low[:, u.slot], raw[:, u.raw], w_high[:, u.slot].bitcast(F32),
                                    ALU.subtract).then_inc(weights_low, 1)

        def product(pe, u, bank, high, low, ready=None, tiles=KD):
            pe.wait_ge(weights_low, u.count(1))
            for k in range(tiles):
                if ready is not None:
                    pe.wait_ge(ready[0], ready[1] + k + 1)
                wh, wl = w_high[:, u.slot, k * P:(k + 1) * P], w_low[:, u.slot, k * P:(k + 1) * P]
                nc.tensor.matmul(bank, wh, high[:, k], start=k == 0, stop=False)
                nc.tensor.matmul(bank, wh, low[:, k], start=False, stop=False)
                mm = nc.tensor.matmul(bank, wl, high[:, k], start=False, stop=k == tiles - 1)
            mm.then_inc(units_done, 1)

        POST_NORM = {R_POST[name] + 1: P_NO[name] for name in names[:-1] if name in P_NO}

        def gathered(r):
            return 6 * (r - sum(q < r for q in POST_NORM))

        def norm_square(act, r, m, src):
            if r in POST_NORM:
                if m == 0:
                    act.wait_ge(norm_summed, 2 * r)
                if m >= 3:
                    act.wait_ge(post_summed, 7 * POST_NORM[r] + m - 2)
                target = (root, sq, ssq)[m % 3]
            else:
                if m >= 3:
                    act.wait_ge(norm_gathered, gathered(r) + m - 2)
                elif m == 2 and r > 0:
                    act.wait_ge(norm_summed, 2 * r)
                target = root if m == 0 else (sq, ssq)[m % 2]
            nc.scalar.activation(target[:], src, ACT.Square).then_inc(norm_squared, 1)

        def norm_gather(pool, r):
            for m in range(1, KD - 1):
                pool.wait_ge(norm_squared, 8 * r + m + 1)
                if m > 1:
                    pool.wait_ge(norm_gathered, gathered(r) + m - 1)
                nc.gpsimd.tensor_tensor(root[:], root[:], (sq, ssq)[m % 2][:], ALU.add).then_inc(norm_gathered, 1)

        def column_sums(buffer, n):
            for b in range(NBLK):
                mm = nc.tensor.matmul(ps[:, 5, NBLK * n + b:NBLK * n + b + 1], buffer[:, b * P:(b + 1) * P], ones[:, 0:1],
                                      start=True, stop=True)
            return mm

        def norm_sum(pe, r):
            if r > 0:
                pe.wait_ge(norm_added, r)
            if r in POST_NORM:
                for m in range(KD):
                    pe.wait_ge(norm_squared, 8 * r + m + 1)
                    nc.tensor.matmul(ps[:, 5], ones, (root, sq, ssq)[m % 3][:], start=m == 0,
                                     stop=m == KD - 1).then_inc(*((post_summed, 1) if m < KD - 1 else (norm_summed, 2)))
                return
            pe.wait_ge(norm_gathered, gathered(r) + 6)
            column_sums(root, 0).then_inc(norm_summed, 1)
            pe.wait_ge(norm_squared, 8 * (r + 1))
            column_sums(ssq, 1).then_inc(norm_summed, 1)
            pe.wait_ge(rstd_done, r + 1)
            for b in range(NBLK):
                mm = nc.tensor.matmul(ps[:, 7, b * P:(b + 1) * P], norm_rstds[:, b:b + 1].to_broadcast([P, P]), ident,
                                      start=True, stop=True)
            mm.then_inc(rstd_spread, 1)

        def norm_root(act, r):
            nc.scalar.activation(norm_spare, con("eps"), ACT.Sqrt)
            if r in POST_NORM:
                act.wait_ge(norm_summed, 2 * (r + 1))
                nc.scalar.activation(rstd[:], ps[:, 5], ACT.Sqrt, scale=1.0 / D, bias=con("eps")).then_inc(root_done, 1)
            else:
                act.wait_ge(norm_added, r + 1)
                nc.scalar.activation(norm_roots, norm_sums, ACT.Sqrt, scale=1.0 / D, bias=con("eps")).then_inc(root_done, 1)

        def norm_rstd(dve, r):
            if r in POST_NORM:
                dve.wait_ge(root_done, r + 1)
                dve.sem_inc(norm_added, 1)
                dve.sem_inc(rstd_done, 1)
                nc.vector.reciprocal(ps[:, 7], rstd[:]).then_inc(rstd_spread, 1)
            else:
                dve.wait_ge(norm_summed, 2 * (r + 1))
                nc.vector.tensor_reduce(norm_sums, ps[:, 5, 0:2 * NBLK].rearrange("p (m b) -> p b m", m=2), AXIS.X,
                                        ALU.add).then_inc(norm_added, 1)
                dve.wait_ge(root_done, r + 1)
                nc.vector.reciprocal(norm_rstds, norm_roots).then_inc(rstd_done, 1)
                if r == 0:
                    split_low(dve, Unit(1))
            dve.wait_ge(rstd_spread, r + 1)

        def by_class(ap):
            return ap.rearrange("q (p r) -> q r p", r=CLASSES)

        def grouped(ap):
            return ap.rearrange("q (r p) -> q r p", r=CLASSES)

        def normalise(dve, r, t, gain, classes=False):
            norm_rstd(dve, r)

            def low(k):
                dve.wait_ge(h_high_done, 8 * t + k + 1)
                nc.vector.tensor_tensor(h_low[:, k], full[:, k % 2], h_high[:, k].bitcast(F32),
                                        ALU.subtract).then_inc(h_low_done, 1)

            for k in range(KD):
                if k >= 2:
                    dve.wait_ge(h_low_done, 8 * t + k - 1)
                xk, rk, fk = x[:, k], ps[:, 7], full[:, k % 2]
                if classes:
                    xk, rk, fk = by_class(xk), by_class(rk), grouped(fk)
                nc.vector.scalar_tensor_tensor(out=fk, in0=xk, scalar=par(gain[0], gain[1] + k), in1=rk,
                                               op0=ALU.mult, op1=ALU.mult).then_inc(h_full, 1)
                if k >= 1:
                    low(k - 1)
            low(KD - 1)

        def normalise_high(act, t):
            for k in range(KD):
                act.wait_ge(h_full, 8 * t + k + 1)
                nc.scalar.activation(h_high[:, k], full[:, k % 2], ACT.Copy).then_inc(h_high_done, 1)

        def rounds(eng, straight, body):
            if straight:
                for i in range(2):
                    body(None, 4 * i)
            else:
                with eng.Fori(0, 2) as i:
                    body(i, 0)

        def out_product(pe, o, first, y_base, tiles=KD, r=None, last=False):
            def body(loop, at):
                per = 4 if loop is not None else 0
                for j in range(4):
                    u = Unit(first + at + j, loop, per)
                    pe.wait_ge(out_free, lin(8 * o + at + j + 1, loop, per))
                    ready = (y_low_done, y_base) if at + j == 0 else None
                    product(pe, u, ps[:, 6 + j % 2], y_high, y_low, ready, tiles)
            rounds(pe, last, body)
            if r is not None:
                norm_sum(pe, r)

        def out_split(act, o, first, target=None, r=None, last=False):
            def body(loop, at):
                for j in range(4):
                    split_high(act, Unit(first + at + j + AHEAD, loop, 4 if loop is not None else 0))
                    if r is not None:
                        act.wait_ge(out_free, 8 * o + at + j + 3)
                        norm_square(act, r, at + j, target[:, at + j])
            rounds(act, last or r is not None, body)
            if r is not None:
                norm_root(act, r)

        def out_take(dve, o, first, target, fresh=False, r=None, classes=False, last=False):
            def body(loop, at):
                per = 4 if loop is not None else 0
                for j in range(4):
                    u = Unit(first + at + j, loop, per)
                    split_low(dve, u + AHEAD)
                    dve.wait_ge(units_done, u.count(1))
                    m = at + j if loop is None else loop * 4 + j
                    tile = target[:, bass.ds(m, 1)].rearrange("q a t -> q (a t)")
                    bank = ps[:, 6 + j % 2]
                    if fresh:
                        ins = nc.vector.tensor_copy(tile, bank)
                    elif classes:
                        ins = nc.vector.tensor_tensor(by_class(tile), by_class(tile), grouped(bank), ALU.add)
                    else:
                        ins = nc.vector.tensor_tensor(tile, tile, bank, ALU.add)
                    ins.then_inc(out_free, 1)
            rounds(dve, last, body)

        a_v = view(0, NBLK, A_WIDTH)
        a_vs = view(8192, 2, NBLK, P)
        a_sz = view(9216, 2, T)
        a_t1 = view(10240, 2, T)
        a_t2 = view(11264, 2, T)
        a_junk = a_t1[:, 0]
        a_vss = view(12288, NBLK, 4)
        a_sum = view(12304, NBLK)
        a_root = view(12308, NBLK)
        a_vr = view(12312, NBLK)
        a_ws = table[:, 0:1024].rearrange("p (g i) -> p g i", g=A_GROUPS)
        a_bs = table[:, 1024:2048].rearrange("p (g i) -> p g i", g=A_GROUPS)
        A_STEPS = 4

        def a_step(a, m, pos, loop=None, per=0):
            return lin(A_STEPS * (A_TILES * a + m + 2) + pos, loop, per * A_STEPS)

        def a_tensor(pe, a, t, first, o, y_base, r, last=False):
            for c in range(4):
                for kk in range(4):
                    u = Unit(first + 4 * c + kk)
                    pe.wait_ge(weights_low, u.count(1))
                    for kl in range(2):
                        k = 2 * kk + kl
                        if c == 0:
                            pe.wait_ge(h_low_done, 8 * t + k + 1)
                        wh = w_high[:, u.slot, kl * T:(kl + 1) * T]
                        wl = w_low[:, u.slot, kl * T:(kl + 1) * T]
                        for b in range(NBLK):
                            if k == 0 and c >= 2:
                                pe.wait_ge(v_copied, 16 * a + 4 * (c - 2) + b + 1)
                            bank = ps[:, 4 * (c % 2) + b]
                            hh, hl = h_high[:, k, b * P:(b + 1) * P], h_low[:, k, b * P:(b + 1) * P]
                            nc.tensor.matmul(bank, hh, wh, start=k == 0, stop=False)
                            nc.tensor.matmul(bank, hh, wl, start=False, stop=False)
                            mm = nc.tensor.matmul(bank, hl, wh, start=False, stop=k == KD - 1)
                    mm.then_inc(units_done, 1)
            pe.wait_ge(v_copied, 16 * a + 12)
            pe.wait_ge(a_masked, a + 1)
            for half in range(2):
                start = first + 16 + 24 * half
                with pe.Fori(0, 4) as i:
                    for j in range(2):
                        m = 8 * half + j
                        pe.wait_ge(a_vector, a_step(a, m - 2, 3, i, 2))
                        product(pe, Unit(start + 2 * j, i, 4), ps[:, j], h_high, h_low)
                        pe.wait_ge(a_silu, lin(16 * a + m + 1, i, 2))
                        product(pe, Unit(start + 2 * j + 1, i, 4), ps[:, 2 + j], h_high, h_low)
                        pe.wait_ge(a_vector, a_step(a, m, 1, i, 2))
                        for c in range(NBLK):
                            ws = a_ws[:, bass.ds(i + 4 * half, 1)].rearrange("p a i -> p (a i)")
                            mm = nc.tensor.matmul(ps[:, 4 + j, c * P:(c + 1) * P], a_vs[:, j, c], ws,
                                                  start=True, stop=True)
                        mm.then_inc(mix_done, 1)
                out_product(pe, o + half, start + 16, y_base + 8 * half, r=r if half == 1 else None, last=last and half == 1)

        def a_scalar(act, a, t, first, o, y_base, r, last=False):
            for c in range(4):
                for kk in range(4):
                    split_high(act, Unit(first + 4 * c + kk + AHEAD))
                for b in range(NBLK):
                    n = 16 * a + 4 * c + b
                    act.wait_ge(v_copied, n + 1)
                    if n > 0:
                        act.wait_ge(v_squared, n)
                    nc.scalar.activation(a_junk, a_v[:, b, c * T:(c + 1) * T], ACT.Square,
                                         accum_out=a_vss[:, b, c:c + 1]).then_inc(v_squared, 1)
            act.wait_ge(v_stats, a + 1)
            nc.scalar.activation(a_root, a_sum, ACT.Sqrt, scale=1.0 / A_WIDTH, bias=con("eps")).then_inc(v_root, 1)
            for half in range(2):
                start = first + 16 + 24 * half
                with act.Fori(0, 4) as i:
                    for j in range(2):
                        m = 8 * half + j
                        u = Unit(start + 2 * j, i, 4)
                        split_high(act, u + AHEAD)
                        split_high(act, u + 1 + AHEAD)
                        act.wait_ge(units_done, u.count(2))
                        act.wait_ge(a_vector, a_step(a, m - 2, 4, i, 2))
                        nc.scalar.activation(a_sz[:, j], ps[:, 2 + j], ACT.Silu).then_inc(a_silu, 1)
                        act.wait_ge(a_vector, a_step(a, m, 4, i, 2))
                        nc.scalar.activation(y_high[:, bass.ds(2 * i + j, 1)], full[:, j:j + 1],
                                             ACT.Copy).then_inc(y_high_done, 1)
                out_split(act, o + half, start + 16, x, r if half == 1 else None, last and half == 1)

        def a_vector_part(dve, name, a, t, first, o, y_base, r, last=False):
            dve.wait_ge(table_loaded, 16 * (TABLED.index(name) + 1))
            causal = con("causal", 0, P).unsqueeze(1).to_broadcast([P, A_GROUPS, P])
            nc.vector.tensor_tensor(a_ws, a_ws, causal, ALU.mult).then_inc(a_masked, 1)
            for c in range(4):
                for kk in range(4):
                    split_low(dve, Unit(first + 4 * c + kk + AHEAD))
                dve.wait_ge(units_done, first + 4 * c + 4)
                for b in range(NBLK):
                    nc.vector.tensor_copy(a_v[:, b, c * T:(c + 1) * T], ps[:, 4 * (c % 2) + b]).then_inc(v_copied, 1)
                if name == "a0" and c < 2 and "o" in names:
                    o_prepare(dve, c)
            dve.wait_ge(v_squared, 16 * (a + 1))
            nc.vector.tensor_reduce(a_sum, a_vss, AXIS.X, ALU.add).then_inc(v_stats, 1)
            dve.wait_ge(v_root, a + 1)
            nc.vector.reciprocal(a_vr, a_root).then_inc(v_stats_r, 1)
            dve.wait_ge(v_stats_r, a + 1)
            for half in range(2):
                start = first + 16 + 24 * half
                with dve.Fori(0, 4) as i:
                    for j in range(2):
                        m = 8 * half + j
                        u = Unit(start + 2 * j, i, 4)
                        tile = bass.ds(i * 2 * P + m * P, P)
                        nc.vector.tensor_tensor(a_vs[:, j], a_v[:, :, tile],
                                                a_vr.unsqueeze(2).to_broadcast([P, NBLK, P]),
                                                ALU.mult).then_inc(a_vector, 1)
                        split_low(dve, u + AHEAD)
                        split_low(dve, u + 1 + AHEAD)
                        dve.wait_ge(mix_done, lin(16 * a + m + 1, i, 2))
                        gain = params[:, bass.ds(i * 2 + (COLUMNS["a_v"] + 16 * a + m), 1)]
                        bias = a_bs[:, bass.ds(i + 4 * half, 1)].to_broadcast([P, NBLK, P])
                        nc.vector.scalar_tensor_tensor(
                            out=a_t1[:, j].rearrange("p (c i) -> p c i", c=NBLK),
                            in0=ps[:, 4 + j].rearrange("p (c i) -> p c i", c=NBLK),
                            scalar=gain, in1=bias, op0=ALU.mult, op1=ALU.add).then_inc(a_vector, 1)
                        dve.wait_ge(a_vector, a_step(a, m, 2, i, 2))
                        nc.vector.tensor_tensor(a_t2[:, j], a_t1[:, j], ps[:, j], ALU.mult).then_inc(a_vector, 1)
                        dve.wait_ge(a_vector, a_step(a, m, 3, i, 2))
                        dve.wait_ge(a_silu, lin(16 * a + m + 3, i, 2))
                        nc.vector.tensor_tensor(full[:, j], a_t2[:, j], a_sz[:, j], ALU.mult).then_inc(a_vector, 1)
                        dve.wait_ge(y_high_done, lin(y_base + m + 1, i, 2))
                        nc.vector.tensor_tensor(y_low[:, bass.ds(2 * i + j, 1)], full[:, j:j + 1],
                                                y_high[:, bass.ds(2 * i + j, 1)].bitcast(F32),
                                                ALU.subtract).then_inc(y_low_done, 1)
                out_take(dve, o + half, start + 16, x, r=r if half == 1 else None, last=last and half == 1)


        BH = 4
        B_TILES = 2 * B_PATTERNS
        B_HALF = 4 * B_PATTERNS + BH * B_TILES + BH
        B_KEYS = T + 2 * P
        b_v = view(0, B_PATTERNS, NBLK, T)
        b_qk = view(6144, 2 * B_TILES - 1, T)
        b_p = view(11776, B_KEYS)
        b_col = view(12544, 64)
        b_pt = work[:, 0:B_KEYS]
        b_o = work[:, B_KEYS:B_KEYS + 3 * T].rearrange("p (h t) -> p h t", h=3)
        b_sq = (sq, ssq)
        b_t2, b_sz = root, rstd
        b_cos, b_sin = table[:, 0:T], table[:, T:2 * T]
        b_strip = table[:, 2 * T:2 * T + 9 * P]
        b_root, b_rk, b_rq = b_col[:, 0:24], b_col[:, 24:36], b_col[:, 36:60]
        b_max, b_neg, b_sum, b_inv = (b_col[:, 60 + n:61 + n] for n in range(4))
        B_SOFT = 7

        def b_tile(j, n):
            return b_qk[:, (j % 2) * (B_TILES - 1) + n if n < B_TILES - 1 else 2 * B_TILES - 2]

        def b_blk(ap, b):
            return ap[:, b * P:(b + 1) * P]

        def b_soft_at(i, j, b, pos):
            return lin(B_SOFT * (NBLK * j + b) + pos, i, B_SOFT * NBLK * BH)

        def b_steps(j, u):
            tile = (j, u - 1) if u > 0 else (j - 1, B_TILES - 1)
            s = (j - 1, u - 1) if 1 <= u <= 4 else None
            t = (j - 1, u - 2) if 2 <= u <= 5 else None
            v = (j - 1, u - 3) if 3 <= u <= 5 else (j - 2, 3) if u == 0 else None
            k = (j, u - 4) if u >= 4 else (j - 1, 2) if u == 0 else None
            return [q if q is not None and 0 <= q[0] < BH else None for q in (tile, s, t, v, k)]

        B_SLOTS = [(j, u) for j in range(BH + 1) for u in range(B_TILES)] + [(BH + 1, 0)]

        def b_unit(first, i, j, u):
            if j > BH or (j == BH and u >= BH):
                return None
            return Unit(first + 4 * B_PATTERNS + B_TILES * j + u, i, B_HALF)

        def b_tensor(pe, t, first, o, y_base, r, last=False):
            pe.wait_ge(out_free, 8 * o + 2)
            with pe.Fori(0, 2) as i:
                pe.wait_ge(y_low_done, lin(y_base, i, BH))
                for g in range(B_PATTERNS):
                    for kk in range(4):
                        u = Unit(first + 4 * g + kk, i, B_HALF)
                        pe.wait_ge(weights_low, u.count(1))
                        for kl in range(2):
                            k = 2 * kk + kl
                            wh = w_high[:, u.slot, kl * T:(kl + 1) * T]
                            wl = w_low[:, u.slot, kl * T:(kl + 1) * T]
                            if g == 0:
                                pe.wait_ge(h_low_done, 8 * t + k + 1)
                            for b in range(NBLK):
                                if k == 0 and g == 2:
                                    pe.wait_ge(b_v_copied, lin(b + 1, i, 12))
                                bank = ps[:, 4 * (g % 2) + b]
                                hh, hl = b_blk(h_high[:, k], b), b_blk(h_low[:, k], b)
                                nc.tensor.matmul(bank, hh, wh, start=k == 0, stop=False)
                                nc.tensor.matmul(bank, hh, wl, start=False, stop=False)
                                mm = nc.tensor.matmul(bank, hl, wh, start=False, stop=k == KD - 1)
                        mm.then_inc(units_done, 1)
                for j, u in B_SLOTS:
                    unit = b_unit(first, i, j, u)
                    tile, s, tr, pv, kn = b_steps(j, u)
                    if unit is not None:
                        n = B_TILES * j + u
                        if n < 2:
                            pe.wait_ge(b_v_copied, lin(9 + n, i, 12))
                        elif j < BH or u < 2:
                            pe.wait_ge(b_gained, lin(n - 1, i, 24))
                        else:
                            pe.wait_ge(b_silu, lin(u - 1, i, BH))
                        product(pe, unit, ps[:, n % 2], h_high, h_low)
                    if tile is not None:
                        n = B_TILES * tile[0] + tile[1]
                        if n == 0:
                            pe.wait_ge(b_v_copied, lin(12, i, 12))
                        if tile[1] == 0 and n > 0:
                            pe.wait_ge(b_root_done, lin(2 * tile[0], i, 2 * BH))
                        if tile[1] == 3:
                            pe.wait_ge(b_root_done, lin(2 * tile[0] + 1, i, 2 * BH))
                        pe.wait_ge(b_gained, lin(n + 1, i, 24))
                        for b in range(NBLK):
                            c = 4 * tile[1] + b
                            mm = nc.tensor.matmul(ps[:, 2, c:c + 1], b_blk(b_sq[n % 2], b), ones[:, 0:1],
                                                  start=True, stop=True)
                        mm.then_inc(b_ss, 1)
                        if n > 0:
                            pe.wait_ge(b_turned, lin(n, i, 24))
                        if tile[1] == 5 or (tile[1] == 0 and n > 0):
                            done = 3 * tile[0] + 2 if tile[1] == 5 else 3 * tile[0]
                            pe.wait_ge(b_k_done, lin(done, i, 12))
                        if tile[1] == 4:
                            pe.wait_ge(b_k_done, lin(3 * tile[0] + 1, i, 12))
                        nc.tensor.matmul(ps[:, 3], con("rot_b", 0, P), b_tile(*tile), start=True,
                                         stop=True).then_inc(b_rot, 1)
                    if pv is not None:
                        j0, b = pv
                        n = NBLK * j0 + b
                        if b == 0 and j0 > 0:
                            pe.wait_ge(b_o_copied, lin(j0, i, 3))
                        pe.wait_ge(b_pt_copied, lin(2 * n + 2, i, 32))
                        for c in range(6):
                            g, kb = (0, c) if c < NBLK else (c - 3, b)
                            mm = nc.tensor.matmul(b_blk(ps[:, 7], b), b_blk(b_v[:, g, kb], j0), b_blk(b_pt, c),
                                                  start=c == 0, stop=c == 5)
                        mm.then_inc(b_pv, 1)
                    if tr is not None:
                        j0, b = tr
                        pe.wait_ge(b_soft, b_soft_at(i, j0, b, 7))
                        nc.tensor.transpose(ps[:, 5, 256:384], b_blk(b_p, 4), ident)
                        nc.tensor.transpose(ps[:, 5, 384:512], b_blk(b_p, 5), ident).then_inc(b_t_few, 1)
                        for c in range(NBLK):
                            mm = nc.tensor.transpose(b_blk(ps[:, 6], c), b_blk(b_p, c), ident)
                        mm.then_inc(b_t_done, 1)
                    if s is not None:
                        j0, b = s
                        n = NBLK * j0 + b
                        pe.wait_ge(b_k_done, lin(3 * j0 + 3, i, 12))
                        pe.wait_ge(b_qk_done, lin(6 * j0 + 6, i, 24))
                        if n > 0:
                            pe.wait_ge(b_soft, b_soft_at(i, j0, b - 1, 3))
                        nc.tensor.matmul(ps[:, 4], b_blk(b_tile(j0, 3), b), b_tile(j0, 0), start=True, stop=True)
                        if n > 0:
                            pe.wait_ge(b_pt_copied, lin(2 * n - 1, i, 32))
                        for g in (1, 2):
                            mm = nc.tensor.matmul(b_blk(ps[:, 5], g - 1), b_blk(b_tile(j0, 3 + g), b),
                                                  b_blk(b_tile(j0, g), b), start=True, stop=True)
                        mm.then_inc(b_scores, 1)
                    if kn is not None:
                        j0, g = kn
                        if u > 0:
                            pe.wait_ge(b_turned, lin(6 * j + u, i, 24))
                        else:
                            pe.wait_ge(b_turned, lin(6 * j, i, 24))
                        pe.wait_ge(b_rk_done, lin(j0 + 1, i, BH))
                        for b in range(NBLK):
                            col = b_rk[:, 4 * g + b:4 * g + b + 1].to_broadcast([P, P])
                            mm = nc.tensor.matmul(b_blk(ps[:, 3], b), col, ident, start=True, stop=True)
                        mm.then_inc(b_spread, 1)
            out_product(pe, o, first + 2 * B_HALF, y_base, r=r, last=last)

        def b_scalar(act, first, o, y_base, r, last=False):
            with act.Fori(0, 2) as i:
                for n in range(4 * B_PATTERNS):
                    split_high(act, Unit(first + n + AHEAD, i, B_HALF))
                for j, u in B_SLOTS:
                    unit = b_unit(first, i, j, u)
                    tile, s, tr, pv, kn = b_steps(j, u)
                    if unit is not None:
                        split_high(act, unit + AHEAD)
                        act.wait_ge(units_done, unit.count(1))
                        n = B_TILES * j + u
                        if j < BH:
                            if n >= 2:
                                act.wait_ge(b_ss, lin(n - 1, i, 24))
                            nc.scalar.activation(b_sq[n % 2][:], ps[:, n % 2], ACT.Square).then_inc(b_squared, 1)
                            if j >= 2 and u < 5:
                                act.wait_ge(b_scores, lin(NBLK * (j - 1), i, 16))
                            if j >= 1 and u == 5:
                                act.wait_ge(b_scores, lin(NBLK * j, i, 16))
                            gain = par("b_k" if u < 3 else "b_q", u % 3)
                            nc.scalar.activation(b_tile(j, u), ps[:, n % 2], ACT.Copy,
                                                 scale=gain).then_inc(b_gained, 1)
                        else:
                            if u > 0:
                                act.wait_ge(b_gated, lin(u, i, BH))
                            nc.scalar.activation(b_sz[:], ps[:, n % 2], ACT.Silu).then_inc(b_silu, 1)
                    if tile is not None and tile[1] in (2, 5):
                        act.wait_ge(b_ss, lin(6 * tile[0] + tile[1] + 1, i, 24))
                        c = 12 * (tile[1] // 3)
                        if tile[1] == 2 and tile[0] > 0:
                            act.wait_ge(b_rk_done, lin(tile[0], i, BH))
                        if tile[1] == 5 and tile[0] > 0:
                            act.wait_ge(b_rq_done, lin(2 * tile[0], i, 2 * BH))
                        nc.scalar.activation(b_root[:, c:c + 12], ps[:, 2, c:c + 12], ACT.Sqrt, scale=1.0 / P,
                                             bias=con("eps")).then_inc(b_root_done, 1)
                    if tr is not None:
                        n = NBLK * tr[0] + tr[1]
                        if n > 0:
                            act.wait_ge(b_pv, lin(n, i, 16))
                        act.wait_ge(b_t_few, lin(n + 1, i, 16))
                        nc.scalar.activation(b_pt[:, T:], ps[:, 5, 256:512], ACT.Copy).then_inc(b_pt_copied, 1)
                        act.wait_ge(b_t_done, lin(n + 1, i, 16))
                        nc.scalar.activation(b_pt[:, 0:T], ps[:, 6], ACT.Copy).then_inc(b_pt_copied, 1)
                    if s is not None:
                        act.wait_ge(b_soft, b_soft_at(i, s[0], s[1], 5))
                        nc.scalar.activation(b_p, b_p, ACT.Exp, bias=b_neg, accum_out=b_sum).then_inc(b_exp, 1)
                    if j == BH and u < 3:
                        act.wait_ge(b_gated, lin(u + 1, i, BH))
                        nc.scalar.activation(y_high[:, bass.ds(4 * i + u, 1)], full[:, u % 2:u % 2 + 1],
                                             ACT.Copy).then_inc(y_high_done, 1)
                act.wait_ge(b_gated, lin(BH, i, BH))
                nc.scalar.activation(y_high[:, bass.ds(4 * i + 3, 1)], full[:, 1:2], ACT.Copy).then_inc(y_high_done, 1)
            out_split(act, o, first + 2 * B_HALF, x, r, last)

        def b_vector(dve, first, o, y_base, r, last=False):
            dve.wait_ge(table_loaded, 16 * (TABLED.index("b") + 1))
            with dve.Fori(0, 2) as i:
                for g in range(B_PATTERNS):
                    for kk in range(4):
                        split_low(dve, Unit(first + 4 * g + kk + AHEAD, i, B_HALF))
                    dve.wait_ge(units_done, Unit(first + 4 * g, i, B_HALF).count(4))
                    for b in range(NBLK):
                        nc.vector.tensor_copy(b_v[:, g, b], ps[:, 4 * (g % 2) + b]).then_inc(b_v_copied, 1)

                def gate(j, source):
                    dve.wait_ge(b_silu, lin(j + 1, i, BH))
                    dve.wait_ge(y_low_done, lin(y_base + j - 1, i, BH))
                    nc.vector.tensor_tensor(full[:, j % 2], source, b_sz[:], ALU.mult).then_inc(b_gated, 1)
                    dve.wait_ge(y_high_done, lin(y_base + j + 1, i, BH))
                    nc.vector.tensor_tensor(y_low[:, bass.ds(4 * i + j, 1)], full[:, j % 2:j % 2 + 1],
                                            y_high[:, bass.ds(4 * i + j, 1)].bitcast(F32),
                                            ALU.subtract).then_inc(y_low_done, 1)

                for j, u in B_SLOTS:
                    unit = b_unit(first, i, j, u)
                    tile, s, tr, pv, kn = b_steps(j, u)
                    if unit is not None:
                        split_low(dve, unit + AHEAD)
                    if tile is not None:
                        n = B_TILES * tile[0] + tile[1]
                        dve.wait_ge(b_rot, lin(n + 1, i, 24))
                        if n > 0:
                            dve.wait_ge(b_qk_done, lin(n, i, 24))
                        nc.vector.tensor_tensor(b_t2[:], ps[:, 3], b_sin, ALU.mult).then_inc(b_turned, 1)
                        dve.wait_ge(b_turned, lin(n + 1, i, 24))
                        dve.wait_ge(b_cosed, lin(n + 1, i, 24))
                        nc.vector.tensor_tensor(b_tile(*tile), b_tile(*tile), b_t2[:], ALU.add).then_inc(b_qk_done, 1)
                    if tile is not None and tile[1] == 2:
                        dve.wait_ge(b_root_done, lin(2 * tile[0] + 1, i, 2 * BH))
                        if tile[0] > 0:
                            dve.wait_ge(b_spread, lin(3 * tile[0], i, 12))
                        nc.vector.reciprocal(b_rk, b_root[:, 0:12]).then_inc(b_rk_done, 1)
                    if tile is not None and tile[1] == 5:
                        dve.wait_ge(b_root_done, lin(2 * tile[0] + 2, i, 2 * BH))
                        nc.vector.reciprocal(b_rq[:, 12:24], b_root[:, 12:24]).then_inc(b_rq_done, 1)
                        dve.wait_ge(b_rq_done, lin(2 * tile[0] + 1, i, 2 * BH))
                        if tile[0] > 0:
                            dve.wait_ge(b_soft, b_soft_at(i, tile[0] - 1, 3, 3))
                        nc.vector.tensor_scalar(b_rq[:, 0:12], b_rq[:, 12:24], P ** -0.5, None,
                                                op0=ALU.mult).then_inc(b_rq_done, 1)
                    if s is not None:
                        j0, b = s
                        n = NBLK * j0 + b
                        dve.wait_ge(b_scores, lin(n + 1, i, 16))
                        dve.wait_ge(b_rq_done, lin(2 * j0 + 2, i, 2 * BH))
                        if n > 0:
                            dve.wait_ge(b_t_done, lin(n, i, 16))
                        for g in range(B_PATTERNS):
                            src = ps[:, 4] if g == 0 else b_blk(ps[:, 5], g - 1)
                            dst = b_p[:, 0:T] if g == 0 else b_blk(b_p, 3 + g)
                            at, width = ((3 - b) * P, T) if g == 0 else ((6 + g) * P, P)
                            nc.vector.scalar_tensor_tensor(
                                out=dst, in0=src, scalar=b_rq[:, 4 * g + b:4 * g + b + 1],
                                in1=b_strip[:, at:at + width], op0=ALU.mult, op1=ALU.add).then_inc(b_soft, 1)
                        dve.wait_ge(b_soft, b_soft_at(i, j0, b, 3))
                        nc.vector.tensor_reduce(b_max, b_p, AXIS.X, ALU.max).then_inc(b_soft, 1)
                        dve.wait_ge(b_soft, b_soft_at(i, j0, b, 4))
                        nc.vector.tensor_scalar(b_neg, b_max, -1.0, None, op0=ALU.mult).then_inc(b_soft, 1)
                        dve.wait_ge(b_exp, lin(n + 1, i, 16))
                        nc.vector.reciprocal(b_inv, b_sum).then_inc(b_soft, 1)
                        dve.wait_ge(b_soft, b_soft_at(i, j0, b, 6))
                        nc.vector.tensor_scalar(b_p, b_p, b_inv, None, op0=ALU.mult).then_inc(b_soft, 1)
                    if kn is not None:
                        j0, g = kn
                        n = 3 * j0 + g
                        dve.wait_ge(b_spread, lin(n + 1, i, 12))
                        dve.wait_ge(b_qk_done, lin(6 * j0 + g + 1, i, 24))
                        nc.vector.tensor_tensor(b_tile(j0, g), b_tile(j0, g), ps[:, 3], ALU.mult).then_inc(b_k_done, 1)
                    if pv is not None and pv[1] == 3 and pv[0] < 3:
                        dve.wait_ge(b_pv, lin(4 * pv[0] + 4, i, 16))
                        nc.vector.tensor_copy(b_o[:, pv[0]], ps[:, 7]).then_inc(b_o_copied, 1)
                    if j == BH and u < 3:
                        dve.wait_ge(b_o_copied, lin(u + 1, i, 3))
                        gate(u, b_o[:, u])
                dve.wait_ge(b_pv, lin(16, i, 16))
                gate(3, ps[:, 7])
            out_take(dve, o, first + 2 * B_HALF, x, r=r, classes=True, last=last)

        def b_gpsimd(pool):
            pool.wait_ge(table_loaded, 16 * (TABLED.index("b") + 1))
            with pool.Fori(0, 2) as i:
                for j in range(BH):
                    for n in range(B_TILES):
                        pool.wait_ge(b_rot, lin(6 * j + n + 1, i, 24))
                        nc.gpsimd.tensor_tensor(b_tile(j, n), b_tile(j, n), b_cos, ALU.mult).then_inc(b_cosed, 1)

        def post_done(p, k):
            return (post_odd if k % 2 else post_even), KD // 2 * p + k // 2 + 1

        def post_vector(dve, r, p, source, gain):
            norm_rstd(dve, r)

            def add(k):
                dve.wait_ge(post_scaled, 8 * p + k + 1)
                nc.vector.tensor_tensor(x[:, k], x[:, k], full[:, 0], ALU.add).then_inc(post_even, 1)

            for k in range(KD):
                if k >= 2:
                    dve.wait_ge(*post_done(p, k - 2))
                nc.vector.scalar_tensor_tensor(out=full[:, k % 2], in0=source[:, k], scalar=par(gain, k), in1=ps[:, 7],
                                               op0=ALU.mult, op1=ALU.mult).then_inc(post_scaled, 1)
                if k % 2:
                    add(k - 1)

        def post_gpsimd(pool, p):
            for k in range(1, KD, 2):
                pool.wait_ge(post_scaled, 8 * p + k + 1)
                nc.gpsimd.tensor_tensor(x[:, k], x[:, k], full[:, 1], ALU.add).then_inc(post_odd, 1)

        def post_scalar(act, r, p):
            for k in range(KD):
                act.wait_ge(*post_done(p, k))
                norm_square(act, r, k, x[:, k])
            norm_root(act, r)

        PAD = 16
        c_sums = view(1024, 2, PAD + T)
        c_window = view(2080, 2, T)
        c_diff = view(3136, 2, T)
        c_edge = view(4160, PAD)
        c_sz = view(4176, 4, T)
        C_POOL = 14

        def c_units(first):
            out, at = [], first
            xs = [at]
            at += 4
            for g in range(C_POOLS):
                z, mix = at, at + 4
                at += 6
                if g + 1 < C_POOLS:
                    xs.append(at)
                    at += 4
                out.append((xs[g], z, mix, at))
                at += 4
            return out

        C_STEPS = 5

        def c_tensor(pe, t, first, o, y_base, r):
            plan = c_units(first)

            def xs(g):
                for m in range(4):
                    if g > 0:
                        pe.wait_ge(c_gated, 4 * (g - 1) + m + 1)
                    ready = (h_low_done, 8 * t) if g == 0 and m == 0 else None
                    product(pe, Unit(plan[g][0] + m), ps[:, m], h_high, h_low, ready)

            xs(0)
            for g in range(C_POOLS):
                for m in range(4):
                    if 4 * g + m >= 2:
                        pe.wait_ge(c_silu, 4 * g + m - 1)
                    product(pe, Unit(plan[g][1] + m), ps[:, 4 + m % 2], h_high, h_low)
                for n in range(2):
                    u = Unit(plan[g][2] + n)
                    pe.wait_ge(weights_low, u.count(1))
                    for d in range(2):
                        m = 2 * n + d
                        for k in range(4):
                            if n == 0 and d == 0:
                                pe.wait_ge(c_diff_low, 4 * g + k + 1)
                            at = k * 256 + d * P
                            wh, wl = w_high[:, u.slot, at:at + P], w_low[:, u.slot, at:at + P]
                            nc.tensor.matmul(ps[:, m], wh, y_high[:, 4 + k], start=k == 0, stop=False)
                            nc.tensor.matmul(ps[:, m], wh, y_low[:, 4 + k], start=False, stop=False)
                            mm = nc.tensor.matmul(ps[:, m], wl, y_high[:, 4 + k], start=False, stop=k == 3)
                    mm.then_inc(units_done, 1)
                if g + 1 < C_POOLS:
                    xs(g + 1)
                for n in range(4):
                    u = Unit(plan[g][3] + n)
                    pe.wait_ge(weights_low, u.count(1))
                    for d in range(2):
                        m = 2 * n + d
                        pe.wait_ge(out_free, 8 * (o + g) + m + 1)
                        for k in range(4):
                            if m == 0:
                                pe.wait_ge(y_low_done, y_base + 4 * g + k + 1)
                            at = k * 256 + d * P
                            wh, wl = w_high[:, u.slot, at:at + P], w_low[:, u.slot, at:at + P]
                            nc.tensor.matmul(ps[:, 6 + d], wh, y_high[:, k], start=k == 0, stop=False)
                            nc.tensor.matmul(ps[:, 6 + d], wh, y_low[:, k], start=False, stop=False)
                            mm = nc.tensor.matmul(ps[:, 6 + d], wl, y_high[:, k], start=False, stop=k == 3)
                    mm.then_inc(units_done, 1)
            if r is not None:
                norm_sum(pe, r)

        def c_scalar(act, first, o, y_base, r):
            plan = c_units(first)

            def xs(g):
                for m in range(4):
                    split_high(act, Unit(plan[g][0] + m + AHEAD))
                    act.wait_ge(c_pool, 1 + C_STEPS * (4 * g + m + 1))
                    nc.scalar.activation(y_high[:, 4 + m], c_diff[:, m % 2], ACT.Copy).then_inc(c_diff_high, 1)

            xs(0)
            for g in range(C_POOLS):
                for m in range(4):
                    split_high(act, Unit(plan[g][1] + m + AHEAD))
                    act.wait_ge(units_done, plan[g][1] + m + 1)
                    if g > 0:
                        act.wait_ge(c_gated, 4 * (g - 1) + m + 1)
                    nc.scalar.activation(c_sz[:, m], ps[:, 4 + m % 2], ACT.Silu).then_inc(c_silu, 1)
                for n in range(2):
                    split_high(act, Unit(plan[g][2] + n + AHEAD))
                    for d in range(2):
                        m = 2 * n + d
                        act.wait_ge(c_gated, 4 * g + m + 1)
                        nc.scalar.activation(y_high[:, m], full[:, m % 2], ACT.Copy).then_inc(y_high_done, 1)
                if g + 1 < C_POOLS:
                    xs(g + 1)
                for n in range(4):
                    split_high(act, Unit(plan[g][3] + n + AHEAD))
                    if g == C_POOLS - 1 and r is not None:
                        for m in (2 * n, 2 * n + 1):
                            act.wait_ge(out_free, 8 * (o + g) + m + 3)
                            norm_square(act, r, m, x[:, m])
            if r is not None:
                norm_root(act, r)

        def c_vector(dve, first, o, y_base):
            plan = c_units(first)
            nc.vector.memset(c_sums[:, :, 0:PAD], 0.0).then_inc(c_pool, 1)

            def xs(g):
                w = POOL_SIZES[g]
                for m in range(4):
                    b, base = m % 2, 1 + C_STEPS * (4 * g + m)
                    split_low(dve, Unit(plan[g][0] + m + AHEAD))
                    dve.wait_ge(units_done, plan[g][0] + m + 1)
                    dve.wait_ge(c_pool, base)
                    if g > 0 or m >= 2:
                        dve.wait_ge(c_diff_low, 4 * g + m - 1)
                    nc.vector.tensor_tensor_scan(c_sums[:, b, PAD:], ones[:, 0:1].to_broadcast([P, T]), ps[:, m], 0.0,
                                                 ALU.mult, ALU.add).then_inc(c_pool, 1)
                    dve.wait_ge(c_pool, base + 1)
                    nc.vector.tensor_tensor(c_window[:, b], c_sums[:, b, PAD:], c_sums[:, b, PAD - w:PAD + T - w],
                                            ALU.subtract).then_inc(c_pool, 1)
                    dve.wait_ge(c_pool, base + 2)
                    nc.vector.scalar_tensor_tensor(out=c_diff[:, b], in0=c_window[:, b], scalar=1.0 / w, in1=ps[:, m],
                                                   op0=ALU.mult, op1=ALU.subtract).then_inc(c_pool, 1)
                    nc.vector.tensor_tensor(c_edge, c_window[:, b, 0:PAD], con("inv_count", PAD * g, PAD),
                                            ALU.mult).then_inc(c_pool, 1)
                    dve.wait_ge(c_pool, base + 4)
                    nc.vector.tensor_tensor(c_diff[:, b, 0:PAD], c_edge, ps[:, m, 0:PAD],
                                            ALU.subtract).then_inc(c_pool, 1)
                    dve.wait_ge(c_diff_high, 4 * g + m + 1)
                    nc.vector.tensor_tensor(y_low[:, 4 + m], c_diff[:, b], y_high[:, 4 + m].bitcast(F32),
                                            ALU.subtract).then_inc(c_diff_low, 1)

            xs(0)
            for g in range(C_POOLS):
                for m in range(4):
                    split_low(dve, Unit(plan[g][1] + m + AHEAD))
                for n in range(2):
                    split_low(dve, Unit(plan[g][2] + n + AHEAD))
                    dve.wait_ge(units_done, plan[g][2] + n + 1)
                    for d in range(2):
                        m = 2 * n + d
                        dve.wait_ge(c_silu, 4 * g + m + 1)
                        if 4 * g + m >= 2:
                            dve.wait_ge(y_low_done, y_base + 4 * g + m - 1)
                        nc.vector.scalar_tensor_tensor(out=full[:, m % 2], in0=ps[:, m],
                                                       scalar=par("c_scale", 4 * g + m), in1=c_sz[:, m],
                                                       op0=ALU.mult, op1=ALU.mult).then_inc(c_gated, 1)
                        dve.wait_ge(y_high_done, y_base + 4 * g + m + 1)
                        nc.vector.tensor_tensor(y_low[:, m], full[:, m % 2], y_high[:, m].bitcast(F32),
                                                ALU.subtract).then_inc(y_low_done, 1)
                if g + 1 < C_POOLS:
                    xs(g + 1)
                for n in range(4):
                    split_low(dve, Unit(plan[g][3] + n + AHEAD))
                    dve.wait_ge(units_done, plan[g][3] + n + 1)
                    for d in range(2):
                        m = 2 * n + d
                        nc.vector.tensor_tensor(x[:, m], x[:, m], ps[:, 6 + d], ALU.add).then_inc(out_free, 1)

        f_y = view(0, KD, T)
        f_sz = view(4096, 2, T)
        FF_TILES = D_FF // P

        def f_tensor(pe, f, t, first, o, y_base, r, last=False):
            at, done = first, 0
            for q, tiles in enumerate(FF_GROUPS):
                with pe.Fori(0, tiles // 2) as i:
                    for j in range(2):
                        n = FF_TILES * f + done + j
                        pe.wait_ge(f_silu, lin(n + 1, i, 2))
                        product(pe, Unit(at + 2 * j, i, 4), ps[:, j], h_high, h_low,
                                (h_low_done, 8 * t) if q == 0 and j == 0 else None)
                        pe.wait_ge(f_full, lin(n + 1, i, 2))
                        product(pe, Unit(at + 2 * j + 1, i, 4), ps[:, 2 + j], h_high, h_low)
                end = q == len(FF_GROUPS) - 1
                out_product(pe, o + q, at + 2 * tiles, y_base + done, tiles, r if end else None, last and end)
                at += 2 * tiles + 8
                done += tiles

        def f_scalar(act, f, first, o, y_base, r, last=False):
            at, done = first, 0
            for q, tiles in enumerate(FF_GROUPS):
                with act.Fori(0, tiles // 2) as i:
                    for j in range(2):
                        n, u = FF_TILES * f + done + j, Unit(at + 2 * j, i, 4)
                        split_high(act, u + AHEAD)
                        act.wait_ge(units_done, u.count(1))
                        act.wait_ge(f_full, lin(n + 1, i, 2))
                        nc.scalar.activation(f_sz[:, j], ps[:, j], ACT.Silu).then_inc(f_silu, 1)
                        split_high(act, u + 1 + AHEAD)
                        act.wait_ge(f_full, lin(n + 3, i, 2))
                        nc.scalar.activation(y_high[:, bass.ds(2 * i + j, 1)], full[:, j:j + 1],
                                             ACT.Copy).then_inc(y_high_done, 1)
                end = q == len(FF_GROUPS) - 1
                out_split(act, o + q, at + 2 * tiles, f_y, r if end else None, last and end)
                at += 2 * tiles + 8
                done += tiles

        def f_vector(dve, f, first, o, y_base, r, last=False):
            at, done = first, 0
            for q, tiles in enumerate(FF_GROUPS):
                with dve.Fori(0, tiles // 2) as i:
                    for j in range(2):
                        n, u = FF_TILES * f + done + j, Unit(at + 2 * j, i, 4)
                        split_low(dve, u + AHEAD)
                        split_low(dve, u + 1 + AHEAD)
                        dve.wait_ge(units_done, u.count(2))
                        dve.wait_ge(f_silu, lin(n + 3, i, 2))
                        dve.wait_ge(y_low_done, lin(y_base + done + j - 1, i, 2))
                        nc.vector.tensor_tensor(full[:, j], f_sz[:, j], ps[:, 2 + j], ALU.mult).then_inc(f_full, 1)
                        dve.wait_ge(y_high_done, lin(y_base + done + j + 1, i, 2))
                        nc.vector.tensor_tensor(y_low[:, bass.ds(2 * i + j, 1)], full[:, j:j + 1],
                                                y_high[:, bass.ds(2 * i + j, 1)].bitcast(F32),
                                                ALU.subtract).then_inc(y_low_done, 1)
                end = q == len(FF_GROUPS) - 1
                out_take(dve, o + q, at + 2 * tiles, f_y, fresh=q == 0, r=r if end else None, last=last and end)
                at += 2 * tiles + 8
                done += tiles

        SANDWICH = {"f0": f_y, "f1": f_y, "e": view(4224, KD, T), "o": view(0, KD, T)}

        E_PLAN = [("a", 0), ("b", 0), ("a", 1), ("b", 1), ("v", 0), ("v", 1), ("v", 2), ("v", 3), ("q", 0), ("q", 1), ("q", 2),
                  ("q", 3), ("a", 2), ("b", 2), ("q", 4), ("q", 5), ("q", 6), ("q", 7), ("a", 3), ("b", 3)]
        E_STEP_OF = {**{21 + n: n for n in range(8)}, **{25 + n: n for n in range(8, 21)}}
        E_SLOTS = 47
        E_BLOCKS = NBLK * DIFF_HEADS

        def e_taps(m, slot, per, count, first=0, end=CONV_WIDTH):
            return {slot + s: (m, first + per * s, min(first + per * s + per, end)) for s in range(count)}

        E_HALF = 19
        E_TAPS = {**e_taps(0, 4, 2, 16), **e_taps(2, 28, 3, 11), **e_taps(3, 40, 5, 4, 0, E_HALF)}
        E_PRODUCTS = {**e_taps(1, 8, 2, 16), **e_taps(3, 40, 3, 4, E_HALF)}
        E_TAPPED = 2 * CONV_WIDTH + E_HALF
        E_ADDED = CONV_WIDTH + CONV_WIDTH - E_HALF
        E_MEAN, E_VAR, E_NORM = 44, 45, 46
        E_Y_CONV, E_Y_HEAD = 4, (0, 1, 2, 3)

        def e_unit(slot):
            return (slot // 2, *E_PLAN[slot // 2]) if slot < 2 * len(E_PLAN) else (None, None, None)

        PADT = CONV_WIDTH - 1
        e_u = view(0, CONV_TILES, PADT + T)
        e_acc = view(2176, CONV_TILES, T)
        e_qk = view(4224, 2 * DIFF_HEADS, T)
        e_yacc = view(4224, KD, T)
        e_v = view(8320, NBLK, T)
        e_p = view(10368, 2, 2, T)
        e_col = view(12416, 384)
        e_wt, e_osb = work[:, 0:T], work[:, 3 * T:4 * T]
        e_prod = work[:, T:3 * T].rearrange("p (s t) -> p s t", s=2)
        e_sg = (root, rstd)
        e_max, e_inv, e_coef, e_neglam = e_col[:, 0:2], e_col[:, 2:3], e_col[:, 3:4], e_col[:, 4:5]
        e_neg = e_col[:, 6:10].rearrange("p (s c) -> p s c", s=2)
        e_lam, e_lsum = e_col[:, 10:12], e_col[:, 12:14]
        e_sum = e_col[:, 16:48].rearrange("p (h b c) -> p h b c", h=DIFF_HEADS, b=NBLK)
        e_sq0, e_arg, e_root, e_rstd = (e_col[:, 48 + 4 * n:52 + 4 * n] for n in range(4))
        e_larg, e_lroot, e_lrstd = (e_col[:, 64 + 4 * n:68 + 4 * n] for n in range(3))
        e_lprod = e_col[:, 96:96 + 2 * DIFF_DIM]
        E_SOFT, E_MIX = 3, 3

        def e_product(m, j):
            return j if m == 1 else CONV_WIDTH + j - E_HALF

        def e_rot_tile(slot):
            at, half = divmod(slot, 2)
            if half == 0 and 1 <= at <= len(E_PLAN) and E_PLAN[at - 1][0] == "q":
                return E_PLAN[at - 1][1]
            return None

        def e_bank(kind, n):
            if kind == "a":
                return (0, 1, 0, 0)[n], ((), (), ((e_raw, 3),), ((e_raw, 8),))[n]
            if kind == "b":
                return (2, 3, 1, 1)[n], ((), (), ((e_turned, 4),), ((e_turned, 8), (e_sub_arg, 4), (e_y_full, 2)))[n]
            return e_qk_bank(n), (((e_gated, 1),), ((e_gated, 2),), ((e_raw, 1),), ((e_raw, 2),), ((e_gated, 3),), ((e_raw, 5),),
                                  ((e_raw, 6),), ((e_raw, 7),))[n]

        def e_bank_b(n):
            return e_bank("b", n)[0]

        def e_qk_bank(n):
            return 1 if n in (1, 3) else 0

        def e_rot_bank(n):
            return 6 if n < 3 else 1

        def e_step(n):
            def block(m):
                return m if 0 <= m < E_BLOCKS else None

            def head(m):
                return m // NBLK if m >= 0 and m % NBLK == 0 else None

            return block(n), block(n - 1), block(n - 2), block(n - 3), head(n - 6), head(n - 7), head(n - 8)

        def e_tensor(pe, t, first, o, y_base, r, last=False):
            pe.wait_ge(out_free, 8 * o + 2)
            turns, sums, spread = 0, 0, 0
            for slot in range(E_SLOTS):
                at, kind, n = e_unit(slot)
                half = slot % 2
                if at is not None:
                    u = Unit(first + at)
                    pe.wait_ge(weights_low, u.count(1))
                if kind == "v":
                    k = 2 * n + half
                    wh, wl = w_high[:, u.slot, half * T:(half + 1) * T], w_low[:, u.slot, half * T:(half + 1) * T]
                    for b in range(NBLK):
                        hh, hl = h_high[:, k, b * P:(b + 1) * P], h_low[:, k, b * P:(b + 1) * P]
                        nc.tensor.matmul(ps[:, 4 + b], hh, wh, start=k == 0, stop=False)
                        nc.tensor.matmul(ps[:, 4 + b], hh, wl, start=False, stop=False)
                        mm = nc.tensor.matmul(ps[:, 4 + b], hl, wh, start=False, stop=k == KD - 1)
                    if half == 1:
                        mm.then_inc(units_done, 1)
                elif kind is not None:
                    bank, waits = e_bank(kind, n)
                    if half == 0:
                        for signal, value in waits:
                            pe.wait_ge(signal, value)
                    for k in range(4 * half, 4 * half + 4):
                        if at == 0:
                            pe.wait_ge(h_low_done, 8 * t + k + 1)
                        wh, wl = w_high[:, u.slot, k * P:(k + 1) * P], w_low[:, u.slot, k * P:(k + 1) * P]
                        nc.tensor.matmul(ps[:, bank], wh, h_high[:, k], start=k == 0, stop=False)
                        nc.tensor.matmul(ps[:, bank], wh, h_low[:, k], start=False, stop=False)
                        mm = nc.tensor.matmul(ps[:, bank], wl, h_high[:, k], start=False, stop=k == KD - 1)
                    if half == 1:
                        mm.then_inc(units_done, 1)
                n = e_rot_tile(slot)
                if n is not None:
                    if n == 0:
                        pe.wait_ge(e_v_copied, 4)
                    pe.wait_ge(e_raw, n + 1)
                    if n > 0:
                        pe.wait_ge(e_turned, n)
                    if n == 4:
                        pe.wait_ge(e_sig, 3)
                    if sums > 0:
                        pe.wait_ge(e_sub_arg, 2 * sums)
                    if spread > 0:
                        pe.wait_ge(e_y_full, spread)
                    nc.tensor.matmul(ps[:, e_rot_bank(n)], con("rot_e", 0, P), e_qk[:, n], start=True,
                                     stop=True).then_inc(e_rot, 1)
                    turns += 1
                if slot in E_STEP_OF:
                    s, w, tr, v, end, summed, norm = e_step(E_STEP_OF[slot])
                    if v is not None:
                        h, b = divmod(v, NBLK)
                        pe.wait_ge(e_wt_copied, v + 1)
                        if b == 0 and h > 0:
                            pe.wait_ge(e_o_copied, 2 * h)
                        for kb in range(b + 1):
                            mm = nc.tensor.matmul(ps[:, 7, b * P:(b + 1) * P], e_v[:, kb, h * P:(h + 1) * P],
                                                  e_wt[:, kb * P:(kb + 1) * P], start=kb == 0, stop=kb == b)
                        mm.then_inc(e_pv, 1)
                    if tr is not None:
                        if tr == 0:
                            pe.wait_ge(e_turned, 3)
                        pe.wait_ge(e_mix, E_MIX * (tr + 1))
                        for kb in range(tr % NBLK + 1):
                            mm = nc.tensor.transpose(ps[:, 6, kb * P:(kb + 1) * P],
                                                     e_p[:, tr % 2, 0, kb * P:(kb + 1) * P], ident)
                        mm.then_inc(e_t_done, 1)
                    if s is not None:
                        h, b = divmod(s, NBLK)
                        pe.wait_ge(e_qk_done, 2 * h + 2)
                        if s == 0:
                            pe.wait_ge(e_sig, 2)
                        elif s >= 2:
                            pe.wait_ge(e_exp, 2 * s - 2)
                        for c in range(2):
                            rows = slice(c * DIFF_DIM, (c + 1) * DIFF_DIM)
                            mm = nc.tensor.matmul(ps[:, 2 + 2 * (s % 2) + c, 0:(b + 1) * P],
                                                  e_qk[rows, 2 * h, b * P:(b + 1) * P],
                                                  e_qk[rows, 2 * h + 1, 0:(b + 1) * P], start=True, stop=True)
                        mm.then_inc(e_scores, 1)
                    if summed is not None:
                        pe.wait_ge(e_o_copied, 2 * summed + 1)
                        pe.wait_ge(e_turned, turns)
                        pe.wait_ge(e_sig, 3 if slot < 40 else 4)
                        if summed > 0:
                            pe.wait_ge(e_y_full, spread)
                        for b in range(NBLK):
                            mm = nc.tensor.matmul(ps[:, 1, b:b + 1], sq[:, b * P:(b + 1) * P], ones[:, 0:1], start=True, stop=True)
                        mm.then_inc(e_sub_sum, 1)
                        sums += 1
                    if norm is not None:
                        pe.wait_ge(e_sub_rstd, norm + 1)
                        pe.wait_ge(e_turned, turns)
                        pe.wait_ge(e_sig, 3 if slot < 40 else 4)
                        for b in range(NBLK):
                            mm = nc.tensor.matmul(ps[:, 1, b * P:(b + 1) * P], e_rstd[:, b:b + 1].to_broadcast([P, P]),
                                                  ident, start=True, stop=True)
                        mm.then_inc(e_sub_spread, 1)
                        spread = E_Y_HEAD[norm] + 1
                if slot == E_MEAN:
                    pe.wait_ge(e_gated, 4)
                    for m in range(CONV_TILES):
                        if m == CONV_TILES - 1:
                            pe.wait_ge(e_joined, 1)
                        mm = nc.tensor.matmul(ps[:, 0], ones, e_acc[:, m], start=m == 0, stop=m == CONV_TILES - 1)
                    mm.then_inc(e_ln_mean, 1)
                if slot == E_VAR:
                    pe.wait_ge(e_centred, CONV_TILES)
                    for m in range(CONV_TILES):
                        pe.wait_ge(e_ln_squared, m + 1)
                        for b in range(NBLK):
                            mm = nc.tensor.matmul(ps[:, 0, NBLK * m + b:NBLK * m + b + 1],
                                                  e_prod[:, m % 2, b * P:(b + 1) * P], ones[:, 0:1], start=True, stop=True)
                        mm.then_inc(e_ln_sum, 1)
                if slot == E_NORM:
                    pe.wait_ge(e_ln_rstd, 2)
                    for b in range(NBLK):
                        mm = nc.tensor.matmul(ps[:, 0, b * P:(b + 1) * P], e_lrstd[:, b:b + 1].to_broadcast([P, P]), ident,
                                              start=True, stop=True)
                    mm.then_inc(e_ln_spread, 1)
            out_product(pe, o, first + len(E_PLAN), y_base, r=r, last=last)

        def e_scalar(act, first, o, y_base, r, last=False):
            def high(k):
                act.wait_ge(e_y_full, k + 1)
                nc.scalar.activation(y_high[:, k], full[:, k % 2], ACT.Copy).then_inc(y_high_done, 1)

            act.wait_ge(e_lam_done, 2)
            nc.scalar.activation(e_lam, e_lsum, ACT.Exp).then_inc(e_lam_exp, 1)
            for slot in range(E_SLOTS):
                at, kind, n = e_unit(slot)
                if at is not None and slot % 2 == 0:
                    split_high(act, Unit(first + at + AHEAD))
                if kind == "b" and slot % 2 == 1:
                    act.wait_ge(units_done, first + at + 1)
                    if n >= 2:
                        act.wait_ge(e_gated, n - 1)
                    nc.scalar.activation(e_sg[n % 2][:], ps[:, e_bank_b(n)], ACT.Sigmoid).then_inc(e_sig, 1)
                if kind == "q" and slot % 2 == 1:
                    act.wait_ge(units_done, first + at + 1)
                    nc.scalar.activation(e_qk[:, n], ps[:, e_qk_bank(n)], ACT.Copy).then_inc(e_raw, 1)
                if slot in E_STEP_OF:
                    s, w, tr, v, end, summed, norm = e_step(E_STEP_OF[slot])
                    if tr is not None:
                        width = (tr % NBLK + 1) * P
                        act.wait_ge(e_t_done, tr + 1)
                        if tr > 0:
                            act.wait_ge(e_pv, tr)
                        nc.scalar.activation(e_wt[:, 0:width], ps[:, 6, 0:width], ACT.Copy).then_inc(e_wt_copied, 1)
                    if end is not None:
                        act.wait_ge(e_pv, v + 1)
                        if end > 0:
                            act.wait_ge(e_sub_sum, end)
                        nc.scalar.activation(sq[:], ps[:, 7], ACT.Square).then_inc(e_o_copied, 1)
                        if end > 0:
                            act.wait_ge(e_y_full, E_Y_HEAD[end - 1] + 1)
                        nc.scalar.activation(e_osb, ps[:, 7], ACT.Copy).then_inc(e_o_copied, 1)
                    if s is not None:
                        h, b = divmod(s, NBLK)
                        width = (b + 1) * P
                        act.wait_ge(e_soft, E_SOFT * (s + 1))
                        for c in range(2):
                            nc.scalar.activation(e_p[:, s % 2, c, 0:width], ps[:, 2 + 2 * (s % 2) + c, 0:width], ACT.Exp,
                                                 bias=e_neg[:, s % 2, c:c + 1], scale=DIFF_DIM ** -0.5,
                                                 accum_out=e_sum[:, h, b, c:c + 1]).then_inc(e_exp, 1)
                    if summed is not None:
                        act.wait_ge(e_sub_arg, 2 * summed + 2)
                        nc.scalar.activation(e_root, e_arg, ACT.Sqrt).then_inc(e_sub_root, 1)
                    if norm is not None:
                        high(E_Y_HEAD[norm])
                if slot in E_PRODUCTS:
                    m, j0, j1 = E_PRODUCTS[slot]
                    act.wait_ge(e_gated, m + 1)
                    for j in range(j0, j1):
                        n = e_product(m, j)
                        if n >= 2:
                            act.wait_ge(e_added, n - 1)
                        nc.scalar.activation(e_prod[:, n % 2], e_u[:, m, j:j + T], ACT.Copy,
                                             scale=par("dw_w", 31 * m + j)).then_inc(e_tapped, 1)
                if slot == E_VAR:
                    for m in range(CONV_TILES):
                        act.wait_ge(e_centred, m + 1)
                        if m >= 2:
                            act.wait_ge(e_ln_sum, m - 1)
                        nc.scalar.activation(e_prod[:, m % 2], e_acc[:, m], ACT.Square).then_inc(e_ln_squared, 1)
                if slot == E_NORM:
                    act.wait_ge(e_ln_rstd, 1)
                    nc.scalar.activation(e_lroot, e_larg, ACT.Sqrt, scale=1.0 / (CONV_TILES * P),
                                         bias=con("ln_eps")).then_inc(e_ln_root, 1)
                    for m in range(CONV_TILES):
                        k = E_Y_CONV + m
                        act.wait_ge(e_ln_scaled, m + 1)
                        act.wait_ge(y_low_done, y_base + k - 1)
                        nc.scalar.activation(full[:, k % 2], e_acc[:, m], ACT.Silu, scale=par("ln_g", m),
                                             bias=par("ln_b", m)).then_inc(e_y_full, 1)
                        high(k)
            out_split(act, o, first + len(E_PLAN), e_yacc, r, last)

        def e_vector(dve, first, o, y_base, r, last=False):
            dve.wait_ge(table_loaded, 16 * (TABLED.index("e") + 1))

            def low(k):
                dve.wait_ge(y_high_done, y_base + k + 1)
                nc.vector.tensor_tensor(y_low[:, k], full[:, k % 2], y_high[:, k].bitcast(F32),
                                        ALU.subtract).then_inc(y_low_done, 1)

            nc.vector.memset(e_u[:, :, 0:PADT], 0.0).then_inc(e_padded, 1)
            lam = par("lambda", 0, 4 * DIFF_DIM).rearrange("p (c q d) -> p c q d", c=2, q=2)
            prod = e_lprod.rearrange("p (c d) -> p c d", c=2)
            nc.vector.tensor_tensor(prod, lam[:, :, 0], lam[:, :, 1], ALU.mult).then_inc(e_lam_done, 1)
            dve.wait_ge(e_lam_done, 1)
            nc.vector.tensor_reduce(e_lsum, prod, AXIS.X, ALU.add).then_inc(e_lam_done, 1)
            dve.wait_ge(e_lam_exp, 1)
            nc.vector.tensor_tensor(e_lsum[:, 0:1], e_lam[:, 1:2], e_lam[:, 0:1], ALU.subtract).then_inc(e_lam_done, 1)
            dve.wait_ge(e_lam_done, 3)
            nc.vector.tensor_scalar(e_neglam, e_lsum[:, 0:1], -LAM_INIT, None, op0=ALU.add).then_inc(e_lam_done, 1)
            for slot in range(E_SLOTS):
                at, kind, n = e_unit(slot)
                if at is not None and slot % 2 == 0:
                    split_low(dve, Unit(first + at + AHEAD))
                if kind == "b" and slot % 2 == 1:
                    dve.wait_ge(e_sig, n + 1)
                    nc.vector.tensor_tensor(e_u[:, n, PADT:], ps[:, e_bank("a", n)[0]], e_sg[n % 2][:],
                                            ALU.mult).then_inc(e_gated, 1)
                if kind == "v" and n == 3 and slot % 2 == 1:
                    dve.wait_ge(units_done, first + at + 1)
                    for b in range(NBLK):
                        nc.vector.tensor_copy(e_v[:, b], ps[:, 4 + b]).then_inc(e_v_copied, 1)
                n = e_rot_tile(slot)
                if n is not None:
                    dve.wait_ge(e_rot, n + 1)
                    if n > 0:
                        dve.wait_ge(e_qk_done, n)
                    nc.vector.tensor_tensor(ssq[:], ps[:, e_rot_bank(n)], table[:, T:2 * T], ALU.mult).then_inc(e_turned, 1)
                    dve.wait_ge(e_turned, n + 1)
                    dve.wait_ge(e_cosed, n + 1)
                    nc.vector.tensor_tensor(e_qk[:, n], e_qk[:, n], ssq[:], ALU.add).then_inc(e_qk_done, 1)
                if slot in E_STEP_OF:
                    s, w, tr, v, end, summed, norm = e_step(E_STEP_OF[slot])
                    if norm is not None:
                        dve.wait_ge(e_sub_root, norm + 1)
                        nc.vector.reciprocal(e_rstd, e_root).then_inc(e_sub_rstd, 1)
                    if s is not None:
                        width = (s % NBLK + 1) * P
                        banks = slice(2 + 2 * (s % 2), 4 + 2 * (s % 2))
                        dve.wait_ge(e_scores, s + 1)
                        nc.vector.memset(ps[0:64, banks, width - 64:width], MASKED).then_inc(e_soft, 1)
                        dve.wait_ge(e_soft, E_SOFT * s + 1)
                        nc.vector.tensor_reduce(e_max, ps[:, banks, 0:width], AXIS.X, ALU.max).then_inc(e_soft, 1)
                        dve.wait_ge(e_soft, E_SOFT * s + 2)
                        if s >= 2:
                            dve.wait_ge(e_exp, 2 * s - 2)
                        nc.vector.tensor_scalar(e_neg[:, s % 2], e_max, -DIFF_DIM ** -0.5, None,
                                                op0=ALU.mult).then_inc(e_soft, 1)
                    if w is not None:
                        h, b = divmod(w, NBLK)
                        width = (b + 1) * P
                        p0, p1 = (e_p[:, w % 2, c, 0:width] for c in range(2))
                        dve.wait_ge(e_exp, 2 * w + 2)
                        nc.vector.reciprocal(e_inv, e_sum[:, h, b, 1:2]).then_inc(e_mix, 1)
                        dve.wait_ge(e_mix, E_MIX * w + 1)
                        dve.wait_ge(e_lam_done, 4)
                        nc.vector.scalar_tensor_tensor(out=e_coef, in0=e_inv, scalar=e_neglam, in1=e_sum[:, h, b, 0:1],
                                                       op0=ALU.mult, op1=ALU.mult).then_inc(e_mix, 1)
                        dve.wait_ge(e_mix, E_MIX * w + 2)
                        nc.vector.scalar_tensor_tensor(out=p0, in0=p1, scalar=e_coef, in1=p0, op0=ALU.mult,
                                                       op1=ALU.add).then_inc(e_mix, 1)
                    if summed is not None:
                        inside = 1.0 / (1 - LAM_INIT) ** 2
                        sum0 = e_sum[:, summed, :, 0]
                        nc.vector.scalar_tensor_tensor(out=e_sq0, in0=sum0, scalar=EPS * inside, in1=sum0, op0=ALU.mult,
                                                       op1=ALU.mult).then_inc(e_sub_arg, 1)
                        dve.wait_ge(e_sub_arg, 2 * summed + 1)
                        dve.wait_ge(e_sub_sum, summed + 1)
                        nc.vector.scalar_tensor_tensor(out=e_arg, in0=ps[:, 1, 0:NBLK], scalar=inside / P, in1=e_sq0,
                                                       op0=ALU.mult, op1=ALU.add).then_inc(e_sub_arg, 1)
                    if norm is not None:
                        k = E_Y_HEAD[norm]
                        dve.wait_ge(e_sub_spread, norm + 1)
                        dve.wait_ge(e_o_copied, 2 * norm + 2)
                        if k >= 2:
                            dve.wait_ge(y_low_done, y_base + k - 1)
                        nc.vector.scalar_tensor_tensor(out=full[:, k % 2], in0=e_osb, scalar=par("subln"), in1=ps[:, 1],
                                                       op0=ALU.mult, op1=ALU.mult).then_inc(e_y_full, 1)
                        low(k)
                if slot in E_TAPS:
                    m, j0, j1 = E_TAPS[slot]
                    for j in range(j0, j1):
                        n = CONV_WIDTH * ((m + 1) // 2) + j
                        if j == 0:
                            dve.wait_ge(e_gated, m + 1)
                        if n > 0:
                            dve.wait_ge(e_tap, n)
                        other = par("dw_b", m).to_broadcast([P, T]) if j == 0 else e_acc[:, m]
                        nc.vector.scalar_tensor_tensor(out=e_acc[:, m], in0=e_u[:, m, j:j + T],
                                                       scalar=par("dw_w", 31 * m + j), in1=other,
                                                       op0=ALU.mult, op1=ALU.add).then_inc(e_tap, 1)
                if slot == E_MEAN:
                    dve.wait_ge(e_added, E_ADDED)
                    dve.wait_ge(e_tap, E_TAPPED)
                    nc.vector.tensor_tensor(e_acc[:, 3], e_acc[:, 3], root[:], ALU.add).then_inc(e_joined, 1)
                    dve.wait_ge(e_joined, 1)
                    dve.wait_ge(e_ln_mean, 1)
                    for m in range(CONV_TILES):
                        nc.vector.scalar_tensor_tensor(out=e_acc[:, m], in0=ps[:, 0], scalar=-1.0 / (CONV_TILES * P),
                                                       in1=e_acc[:, m], op0=ALU.mult, op1=ALU.add).then_inc(e_centred, 1)
                if slot == E_NORM:
                    dve.wait_ge(e_ln_sum, CONV_TILES)
                    nc.vector.tensor_reduce(e_larg, ps[:, 0, 0:CONV_TILES * NBLK].rearrange("p (m b) -> p b m", m=CONV_TILES),
                                            AXIS.X, ALU.add).then_inc(e_ln_rstd, 1)
                    dve.wait_ge(e_ln_root, 1)
                    nc.vector.reciprocal(e_lrstd, e_lroot).then_inc(e_ln_rstd, 1)
                    dve.wait_ge(e_ln_spread, 1)
                    dve.wait_ge(e_ln_squared, CONV_TILES)
                    for m in range(CONV_TILES):
                        nc.vector.tensor_tensor(e_acc[:, m], e_acc[:, m], ps[:, 0], ALU.mult).then_inc(e_ln_scaled, 1)
                    for m in range(CONV_TILES):
                        low(E_Y_CONV + m)
            out_take(dve, o, first + len(E_PLAN), e_yacc, fresh=True, r=r, last=last)

        def e_gpsimd(pool):
            pool.wait_ge(table_loaded, 16 * (TABLED.index("e") + 1))
            pool.wait_ge(zero_done, 1)
            for slot in range(E_SLOTS):
                n = e_rot_tile(slot)
                if n is not None:
                    pool.wait_ge(e_rot, n + 1)
                    nc.gpsimd.tensor_tensor(e_qk[:, n], e_qk[:, n], table[:, 0:T], ALU.mult).then_inc(e_cosed, 1)
                if slot in E_PRODUCTS:
                    m, j0, j1 = E_PRODUCTS[slot]
                    acc = e_acc[:, m] if m < 3 else root[:]
                    for j in range(j0, j1):
                        n = e_product(m, j)
                        pool.wait_ge(e_tapped, n + 1)
                        if n > 0:
                            pool.wait_ge(e_added, n)
                        other = acc
                        if j == 0:
                            other = par("dw_b", m).to_broadcast([P, T])
                        elif j == E_HALF and m == 3:
                            other = norm_zero.to_broadcast([P, T])
                        nc.gpsimd.tensor_tensor(acc, e_prod[:, n % 2], other, ALU.add).then_inc(e_added, 1)

        O_SSM, O_BANKS, O_PER_STEP = 14, 5, 4
        O_STEPS = NBLK * MLA_HEADS + 3

        def o_events():
            out = [("u", 0), ("u", 1), ("bu", 0), ("state", 8), ("u", 2), ("bu", 1), ("state", 14), ("u", 3), ("sum", 0),
                   ("cy", 0), ("state", 22), ("u", 4), ("bu", 2), ("state", 28), ("u", 5), ("cy", 1), ("sum", 1), ("norm", 0),
                   ("state", 36), ("kn", 0), ("v", 0), ("bu", 3), ("uq", 0), ("state", 42), ("uq", 1), ("cy", 2)]
            at, next_bu, next_cy, taken = 3 * O_SSM, 4, 3, 0
            for n in range(O_STEPS):
                out += [("step", n)]
                if next_bu < SSM_TILES and at >= O_SSM * (next_bu - 1) + O_BANKS:
                    out += [("bu", next_bu)]
                    next_bu += 1
                if next_cy < SSM_TILES and at >= O_SSM * (next_cy + 1):
                    out += [("cy", next_cy)]
                    next_cy += 1
                    if next_cy % 4 == 0:
                        out += [("take", taken)]
                        taken += 1
                if n > 0 and at < O_SSM * SSM_TILES:
                    at = min(at + O_PER_STEP, O_SSM * SSM_TILES)
                    out += [("state", at)]
                if n == 2 * NBLK - 1:
                    out += [("uq", 2)]
                if n == O_BLOCKS:
                    out += [("gelu", 0)]
            return out[:-1] + [("glu", 0), out[-1], ("gate", 0)]

        O_IN, O_KN, O_VN, O_UQ, O_GLU, O_OUT = 0, 6, 7, 8, 11, 12
        O_BLOCKS = NBLK * MLA_HEADS
        O_WIDE = MLA_HEADS * P
        O_Y_HEAD, O_Y_SSM = (0, 1, 2, 3, 4, 5), 6
        O_Q_LIN = (20, 23, 26)
        POWERS, EA, EB = 9, 16, 32
        assert 2 ** POWERS == T and EA * EB == T
        o_kn = view(0, MLA_HEADS, T)
        o_yacc = view(0, KD, T)
        o_v = view(3072, NBLK, O_WIDE)
        o_kr = view(6144, T)
        o_q = view(6656, 2, 3, T)
        o_lat = view(6656, 3, T)
        o_us = view(9728, 2, T)
        o_e = view(10752, 2, 2, T)
        o_sg = o_e[:, 0]
        o_wt = work[:, 0:T]
        o_b = work[:, 512:1024].rearrange("p (g c s) -> p g c s", g=2, c=2)
        o_c = work[:, 1024:1536].rearrange("p (c j h) -> p c j h", c=2, j=SSM_TILES)
        o_tmp = work[:, 1536:2048]
        o_ea = work[:, 2048:2304].rearrange("p (c j n) -> p c j n", c=2, j=SSM_TILES)
        o_eb = sq[:].rearrange("p (c j n) -> p c j n", c=2, j=SSM_TILES)
        o_p = table[:, 2 * T:4 * T].rearrange("p (s t) -> p s t", s=2)
        o_a, o_s, o_w = root, rstd, ssq
        o_col = table[:, 4 * T:4 * T + 24]
        o_max = o_col[:, 0:1]
        o_neg, o_sum, o_inv = ([o_col[:, 2 * n + q:2 * n + q + 1] for q in range(2)] for n in range(1, 4))
        o_roots2, o_rstds2 = ([o_col[:, 8 + 8 * n + 4 * q:12 + 8 * n + 4 * q] for q in range(2)] for n in range(2))
        o_mag, o_f, o_sin, o_cos = small[:, 0:8], small[:, 8:24], small[:, 24:96], small[:, 96:168]
        o_x72, o_k72 = view(12320, 72), view(12392, 72)
        o_c8 = [view(12464 + 8 * n, 8) for n in range(10)]
        LN2_1, LN2_2 = 0.693359375, float(np.log(2.0)) - 0.693359375
        O_SOFT = 3
        O_EVENTS = o_events()
        TURN = 2 * np.pi
        TURN_1 = 6.28125
        TURN_2 = float(np.round((TURN - TURN_1) * 2 ** 18) / 2 ** 18)
        TURN_3 = TURN - TURN_1 - TURN_2
        ROUND = 1.5 * 2 ** 23

        def o_step(n):
            s, w, t, v = (m if 0 <= m < O_BLOCKS else None for m in (n, n - 1, n - 2, n - 3))
            end = v // NBLK if v is not None and v % NBLK == NBLK - 1 else None
            return s, w, t, v, end

        def o_bank(n):
            return n % 2 if n < O_Q_LIN[2] else 0

        def o_turn_bank(n):
            return o_bank(O_Q_LIN[n] + 3) if n < 2 else 0

        def o_pv_bank(h):
            return 7 if h < 2 or h % 2 else 0

        def o_score_bank(n):
            return 1 if n % 2 else 5

        def o_tensor(pe, t, first, o, y_base, r, last=False):
            def wait_lin(n):
                if n >= 2:
                    pe.wait_ge(o_lin, n - 1 if n < O_Q_LIN[2] else n)

            def three(bank, slot, cols, k, start, stop):
                wh, wl = w_high[:, slot, cols:cols + P], w_low[:, slot, cols:cols + P]
                nc.tensor.matmul(bank, wh, h_high[:, k], start=start, stop=False)
                nc.tensor.matmul(bank, wh, h_low[:, k], start=False, stop=False)
                return nc.tensor.matmul(bank, wl, h_high[:, k], start=False, stop=stop)

            def turn(n, bank, tile):
                nc.tensor.matmul(bank, con("rot_o", 0, P), tile, start=True, stop=True).then_inc(o_rot, 1)

            pe.wait_ge(out_free, 8 * o + 2)
            for event, n in O_EVENTS:
                if event == "u":
                    wait_lin(n)
                    product(pe, Unit(first + n), ps[:, n % 2], h_high, h_low, (h_low_done, 8 * t) if n == 0 else None)
                if event == "bu":
                    if n == 0:
                        pe.wait_ge(o_lin, 2)
                        pe.wait_ge(ssm_loaded, 16)
                    else:
                        pe.wait_ge(o_ssm, O_SSM * (n - 1) + O_BANKS)
                    rows = slice(32 * (n % 4), 32 * (n % 4) + 32)
                    for c in range(2):
                        mm = nc.tensor.matmul(ps[:, 2 + c], o_b[rows, n // 4, c], o_us[rows, n // 4], start=True,
                                              stop=True, tile_position=(32 * (n % 4), 0))
                    mm.then_inc(o_bu, 1)
                if event == "cy":
                    m = n
                    pe.wait_ge(o_ssm, O_SSM * (m + 1))
                    if m == 0:
                        pe.wait_ge(o_c_done, 6)
                    if m == 4:
                        pe.wait_ge(o_taken, 1)
                    out = ps[32 * (m % 4):32 * (m % 4) + 32, 4]
                    for c in range(2):
                        mm = nc.tensor.matmul(out, o_c[:, c, m], full[:, c], start=c == 0, stop=c == 1,
                                              tile_position=(0, 32 * (m % 4)))
                    mm.then_inc(o_cy, 1)
                if event == "sum":
                    pe.wait_ge(o_squared, 1 if n == 0 else 3)
                    tiles = (0,) if n == 0 else (1, 2)
                    for b in range(NBLK):
                        for m in tiles:
                            mm = nc.tensor.matmul(ps[:, 5 + n, b:b + 1], o_kn[:, m, b * P:(b + 1) * P], ones[:, 0:1],
                                                  start=m == tiles[0], stop=m == tiles[-1])
                    mm.then_inc(o_sums, 1)
                if event == "norm":
                    for q in range(2):
                        pe.wait_ge(o_rstds, q + 1)
                        for b in range(NBLK):
                            mm = nc.tensor.matmul(ps[:, 5 + q, b * P:(b + 1) * P],
                                                  o_rstds2[q][:, b:b + 1].to_broadcast([P, P]), ident, start=True, stop=True)
                        mm.then_inc(o_spread, 1)
                    pe.wait_ge(o_lin, 6)
                    turn(0, ps[:, 7], o_kr)
                if event == "kn":
                    u = Unit(first + O_KN)
                    pe.wait_ge(weights_low, u.count(1))
                    pe.wait_ge(o_n_low, 1)
                    for h in range(MLA_HEADS):
                        wait_lin(6 + h)
                        mm = three(ps[:, h % 2], u.slot, h * P, 2, True, True)
                        mm.then_inc(o_small if h < MLA_HEADS - 1 else units_done, 1)
                if event == "v":
                    u = Unit(first + O_VN)
                    pe.wait_ge(weights_low, u.count(1))
                    for b in range(NBLK):
                        hh, hl = h_high[:, 2, b * P:(b + 1) * P], h_low[:, 2, b * P:(b + 1) * P]
                        for c, (c0, c1) in enumerate(((0, T), (T, O_WIDE))):
                            lin_n = 12 + 2 * b + c
                            wait_lin(lin_n)
                            bank = ps[:, lin_n % 2, 0:c1 - c0]
                            wh, wl = w_high[:, u.slot, c0:c1], w_low[:, u.slot, c0:c1]
                            nc.tensor.matmul(bank, hh, wh, start=True, stop=False)
                            nc.tensor.matmul(bank, hh, wl, start=False, stop=False)
                            mm = nc.tensor.matmul(bank, hl, wh, start=False, stop=True)
                            mm.then_inc(o_small if lin_n < 19 else units_done, 1)
                if event == "uq":
                    u = Unit(first + O_UQ + n)
                    pe.wait_ge(weights_low, u.count(1))
                    pe.wait_ge(o_n_low, 3)
                    for m in range(3):
                        lin_n = O_Q_LIN[n] + m
                        wait_lin(lin_n)
                        if m == 0 and n > 0:
                            pe.wait_ge(o_turned, n + 1)
                        for k in range(2):
                            mm = three(ps[:, o_bank(lin_n)], u.slot, k * 512 + m * P, k, k == 0, k == 1)
                        mm.then_inc(o_small if m < 2 else units_done, 1)
                    pe.wait_ge(o_lin, O_Q_LIN[n] + 3)
                    turn(n + 1, ps[:, o_turn_bank(n)], o_q[:, n % 2, 2])
                if event == "step":
                    s, w, tr, v, end = o_step(n)
                    if v is not None:
                        h, b = divmod(v, NBLK)
                        pe.wait_ge(o_wt_copied, v + 1)
                        if b == 0 and h > 0 and h != 2:
                            pe.wait_ge(y_low_done, y_base + O_Y_HEAD[max(h - 2, 0)] + 1)
                        if v == 0:
                            pe.wait_ge(o_turned, 1)
                        if b == 0 and h == 2:
                            pe.wait_ge(o_turned, 4)
                        for kb in range(b + 1):
                            mm = nc.tensor.matmul(ps[:, o_pv_bank(h), b * P:(b + 1) * P], o_v[:, kb, h * P:(h + 1) * P],
                                                  o_wt[:, kb * P:(kb + 1) * P], start=kb == 0, stop=kb == b)
                        mm.then_inc(o_pv, 1)
                    if tr is not None:
                        pe.wait_ge(o_scaled, tr + 1)
                        for kb in range(tr % NBLK + 1):
                            mm = nc.tensor.transpose(ps[:, 6, kb * P:(kb + 1) * P],
                                                     o_p[:, tr % 2, kb * P:(kb + 1) * P], ident)
                        mm.then_inc(o_t_done, 1)
                    if s is not None:
                        h, b = divmod(s, NBLK)
                        q = o_q[:, h // 2 % 2]
                        pe.wait_ge(o_roped, h // 2 + 2)
                        if s == 0:
                            pe.wait_ge(o_normed, 3)
                        elif s == 1:
                            pe.wait_ge(o_lin, O_Q_LIN[2])
                        else:
                            pe.wait_ge(o_exp, s - 1)
                        rows = slice(64 * (h % 2), 64 * (h % 2) + 64)
                        bank = ps[:, o_score_bank(s), 0:(b + 1) * P]
                        nc.tensor.matmul(bank, q[:, h % 2, b * P:(b + 1) * P], o_kn[:, h, 0:(b + 1) * P], start=True, stop=False)
                        nc.tensor.matmul(bank, q[rows, 2, b * P:(b + 1) * P], o_kr[rows, 0:(b + 1) * P], start=False,
                                         stop=True).then_inc(o_scores, 1)
                if event == "glu":
                    u = Unit(first + O_GLU)
                    pe.wait_ge(weights_low, u.count(1))
                    pe.wait_ge(o_z_low, 2)
                    for m in range(2):
                        for k in range(2):
                            mm = three(ps[:, 2 + m], u.slot, k * 256 + m * P, 3 + k, k == 0, k == 1)
                        mm.then_inc(o_small if m < 1 else units_done, 1)
            out_product(pe, o, first + O_OUT, y_base, r=r, last=last)

        def o_scalar(act, first, o, y_base, r, last=False):
            def copy(target, lin_n, wait, width=T):
                act.wait_ge(*wait)
                nc.scalar.activation(target, ps[:, o_bank(lin_n), 0:width], ACT.Copy).then_inc(o_lin, 1)

            act.dma_start(work[:, 512:1536], ssm_in).then_inc(ssm_loaded, 16)
            lin_small = 0
            for event, n in O_EVENTS:
                if event == "u":
                    u = Unit(first + n)
                    split_high(act, u + AHEAD)
                    act.wait_ge(units_done, u.count(1))
                    if 2 <= n <= 4:
                        nc.scalar.activation(o_kn[:, n - 2], ps[:, n % 2], ACT.Square).then_inc(o_squared, 1)
                    target = (o_us[:, 0], o_us[:, 1], o_lat[:, 0], o_lat[:, 1], o_lat[:, 2], o_kr)[n]
                    copy(target, n, (units_done, u.count(1)))
                if event == "sum":
                    act.wait_ge(o_sums, n + 1)
                    nc.scalar.activation(o_roots2[n], ps[:, 5 + n, 0:NBLK], ACT.Sqrt, scale=(1.0 / P, 0.5 / P)[n],
                                         bias=con("eps")).then_inc(o_roots, 1)
                if event == "norm":
                    act.wait_ge(units_done, first + 6)
                    for m in range(3):
                        act.wait_ge(o_normed, m + 1)
                        nc.scalar.activation(h_high[:, (2, 0, 1)[m]], o_lat[:, m], ACT.Copy).then_inc(o_n_high, 1)
                if event == "kn":
                    u = Unit(first + O_KN)
                    split_high(act, u + AHEAD)
                    act.wait_ge(o_normed, 3)
                    for h in range(MLA_HEADS):
                        lin_small += h < MLA_HEADS - 1
                        copy(o_kn[:, h], 6 + h, (o_small, lin_small) if h < MLA_HEADS - 1 else (units_done, u.count(1)))
                if event == "v":
                    u = Unit(first + O_VN)
                    split_high(act, u + AHEAD)
                    for b in range(NBLK):
                        for c, (c0, c1) in enumerate(((0, T), (T, O_WIDE))):
                            lin_n = 12 + 2 * b + c
                            lin_small += lin_n < 19
                            copy(o_v[:, b, c0:c1], lin_n, (o_small, lin_small) if lin_n < 19 else (units_done, u.count(1)), c1 - c0)
                if event == "uq":
                    u = Unit(first + O_UQ + n)
                    split_high(act, u + AHEAD)
                    act.wait_ge(o_n_low, 3)
                    if n == 2:
                        act.wait_ge(o_scores, 2 * NBLK)
                    for m in range(3):
                        lin_small += m < 2
                        copy(o_q[:, n % 2, m], O_Q_LIN[n] + m, (o_small, lin_small) if m < 2 else (units_done, u.count(1)))
                if event == "step":
                    s, w, tr, v, end = o_step(n)
                    if tr is not None:
                        width = (tr % NBLK + 1) * P
                        act.wait_ge(o_t_done, tr + 1)
                        if tr > 0:
                            act.wait_ge(o_pv, tr)
                        nc.scalar.activation(o_wt[:, 0:width], ps[:, 6, 0:width], ACT.Copy).then_inc(o_wt_copied, 1)
                    if end is not None:
                        act.wait_ge(o_pv, v + 1)
                        nc.scalar.activation(y_high[:, O_Y_HEAD[end]], ps[:, o_pv_bank(end)], ACT.Copy).then_inc(y_high_done, 1)
                    if w is not None:
                        width = (w % NBLK + 1) * P
                        p = o_p[:, w % 2, 0:width]
                        act.wait_ge(o_inverse, w + 1)
                        nc.scalar.activation(p, p, ACT.Copy, scale=o_inv[w % 2]).then_inc(o_scaled, 1)
                    if s is not None:
                        width = (s % NBLK + 1) * P
                        act.wait_ge(o_soft, O_SOFT * (s + 1))
                        nc.scalar.activation(o_p[:, s % 2, 0:width], ps[:, o_score_bank(s), 0:width], ACT.Exp,
                                             bias=o_neg[s % 2], scale=192 ** -0.5, accum_out=o_sum[s % 2]).then_inc(o_exp, 1)
                if event == "gelu":
                    for m in range(2):
                        act.wait_ge(o_taken, m + 1)
                        nc.scalar.activation(o_us[:, m], o_us[:, m], ACT.Gelu_apprx_tanh).then_inc(o_gelu, 1)
                    for m in range(2):
                        act.wait_ge(o_gelu, m + 1)
                        nc.scalar.activation(h_high[:, 3 + m], o_us[:, m], ACT.Copy).then_inc(o_z_high, 1)
                if event == "glu":
                    u = Unit(first + O_GLU)
                    split_high(act, u + AHEAD)
                    act.wait_ge(units_done, u.count(1))
                    act.wait_ge(o_ssm, O_SSM * SSM_TILES)
                    for m in range(2):
                        nc.scalar.activation(o_sg[:, m], ps[:, 2 + m], ACT.Sigmoid, bias=par("glu_b", m)).then_inc(o_sig, 1)
                if event == "gate":
                    for m in range(2):
                        act.wait_ge(o_gated, m + 1)
                        nc.scalar.activation(y_high[:, O_Y_SSM + m], full[:, m], ACT.Copy).then_inc(y_high_done, 1)
            out_split(act, o, first + O_OUT, o_yacc, r, last)

        prepared = [0]

        def o_prepare(dve, part):
            def step(ins):
                ins.then_inc(o_prep, 1)
                prepared[0] += 1
                dve.wait_ge(o_prep, prepared[0])

            def tt(out, a, b, op):
                step(nc.vector.tensor_tensor(out, a, b, op))

            def ts(out, a, s1, op0, s2=None, op1=None):
                if op1 is None:
                    step(nc.vector.tensor_scalar(out, a, s1, None, op0=op0))
                else:
                    step(nc.vector.tensor_scalar(out, a, s1, s2, op0=op0, op1=op1))

            def stt(out, a, s, b, op0, op1):
                step(nc.vector.scalar_tensor_tensor(out=out, in0=a, scalar=s, in1=b, op0=op0, op1=op1))

            def series(out, z, coefficients):
                ts(out, z, coefficients[-1], ALU.mult)
                for c in coefficients[-2::-1]:
                    stt(out, out, c, z, ALU.add, ALU.mult)

            def exponential(out, y, k, p):
                ts(k, y, 1.0 / np.log(2.0), ALU.mult, ROUND, ALU.add)
                ts(k, k, -ROUND, ALU.add)
                ts(k, k, -126.0, ALU.max, 127.0, ALU.min)
                stt(out, k, -LN2_1, y, ALU.mult, ALU.add)
                stt(out, k, -LN2_2, out, ALU.mult, ALU.add)
                ts(out, out, -1.0, ALU.max, 1.0, ALU.min)
                series(p, out, [1.0 / math.factorial(n) for n in range(1, 9)])
                ts(k, k, 127.0, ALU.add, 2.0 ** 23, ALU.mult)
                step(nc.vector.tensor_copy(out.bitcast(I32), k))
                stt(out, p, 1.0, out, ALU.add, ALU.mult)

            a_re, a_im = par("a_re", 0, 8), par("a_im", 0, 8)
            dt, y, k, p, ab_re, ab_im, den, inv, t1, t2 = o_c8
            if part == 0:
                exponential(dt, par("log_dt", 0, 8), k, p)
                tt(y, a_re, dt, ALU.mult)
                exponential(o_mag, y, k, p)
                return
            tt(o_x72[:, 0:8], a_im, dt, ALU.mult)
            for n, size in ((1, 1), (2, 2), (4, 4), (8, 1)):
                ts(o_x72[:, 8 * n:8 * (n + size)], o_x72[:, 0:8 * size], float(2 ** n), ALU.mult)
            ts(o_k72, o_x72, 1.0 / TURN, ALU.mult, ROUND, ALU.add)
            ts(o_k72, o_k72, -ROUND, ALU.add)
            for part in (TURN_1, TURN_2, TURN_3):
                stt(o_x72, o_k72, -part, o_x72, ALU.mult, ALU.add)
            ts(o_x72, o_x72, 0.5, ALU.mult)
            tt(o_k72, o_x72, o_x72, ALU.mult)
            series(o_sin, o_k72, [(-1.0) ** n / math.factorial(2 * n + 1) for n in range(1, 8)])
            stt(o_sin, o_sin, 1.0, o_x72, ALU.add, ALU.mult)
            series(o_cos, o_k72, [(-1.0) ** n / math.factorial(2 * n) for n in range(1, 8)])
            stt(o_x72, o_cos, 1.0, o_sin, ALU.add, ALU.mult)
            stt(o_cos, o_sin, -2.0, o_sin, ALU.mult, ALU.mult)
            ts(o_cos, o_cos, 1.0, ALU.add)
            ts(o_sin, o_x72, 2.0, ALU.mult)
            tt(ab_re, o_mag, o_cos[:, 0:8], ALU.mult)
            ts(ab_re, ab_re, -1.0, ALU.add)
            tt(ab_im, o_mag, o_sin[:, 0:8], ALU.mult)
            tt(den, a_re, a_re, ALU.mult)
            tt(t1, a_im, a_im, ALU.mult)
            tt(den, den, t1, ALU.add)
            step(nc.vector.reciprocal(inv, den))
            for part, (first, second, op) in enumerate(((a_re, a_im, ALU.add), (a_im, a_re, ALU.subtract))):
                if part == 0:
                    tt(t1, ab_re, first, ALU.mult)
                    tt(t2, ab_im, second, ALU.mult)
                else:
                    tt(t1, ab_im, second, ALU.mult)
                    tt(t2, ab_re, first, ALU.mult)
                tt(t1, t1, t2, op)
                tt(o_f[:, 8 * part:8 * part + 8], t1, inv, ALU.mult)
            dve.sem_inc(o_prepared, 1)

        def o_vector(dve, first, o, y_base, r, last=False):
            def low(k, value):
                dve.wait_ge(y_high_done, y_base + k + 1)
                nc.vector.tensor_tensor(y_low[:, k], value, y_high[:, k].bitcast(F32), ALU.subtract).then_inc(y_low_done, 1)

            def rope(n, bank, tile):
                dve.wait_ge(o_rot, n + 1)
                nc.vector.tensor_tensor(o_w[:], bank, table[:, T:2 * T], ALU.mult).then_inc(o_turned, 1)
                nc.vector.tensor_tensor(tile, tile, table[:, 0:T], ALU.mult).then_inc(o_cosed, 1)
                dve.wait_ge(o_turned, n + 1)
                dve.wait_ge(o_cosed, n + 1)
                nc.vector.tensor_tensor(tile, tile, o_w[:], ALU.add).then_inc(o_roped, 1)
                dve.wait_ge(o_roped, n + 1)

            dve.wait_ge(table_loaded, 16 * (TABLED.index("o") + 1))
            def prepare_c():
                dve.wait_ge(ssm_loaded, 16)
                wide = [P, SSM_TILES, 32]
                fr, fi = (f.unsqueeze(2).to_broadcast(wide) for f in (o_f[:, 0:8], o_f[:, 8:16]))
                w1, w2 = (o_w[:, 256 * c:256 * c + 256].rearrange("p (j h) -> p j h", j=SSM_TILES) for c in range(2))
                nc.vector.tensor_tensor(w1, o_c[:, 0], fi, ALU.mult).then_inc(o_c_done, 1)
                nc.vector.tensor_tensor(w2, o_c[:, 1], fi, ALU.mult).then_inc(o_c_done, 1)
                dve.wait_ge(o_c_done, 2)
                nc.vector.tensor_tensor(o_c[:, 0], o_c[:, 0], fr, ALU.mult).then_inc(o_c_done, 1)
                nc.vector.tensor_tensor(o_c[:, 1], o_c[:, 1], fr, ALU.mult).then_inc(o_c_done, 1)
                dve.wait_ge(o_c_done, 4)
                nc.vector.tensor_tensor(o_c[:, 0], o_c[:, 0], w2, ALU.subtract).then_inc(o_c_done, 1)
                nc.vector.scalar_tensor_tensor(out=o_c[:, 1], in0=o_c[:, 1], scalar=-1.0, in1=w1, op0=ALU.mult,
                                               op1=ALU.subtract).then_inc(o_c_done, 1)
                dve.wait_ge(o_c_done, 6)

            def op(j, out, a, b, op, wait):
                if O_SSM * j + wait > 0:
                    dve.wait_ge(o_ssm, O_SSM * j + wait)
                nc.vector.tensor_tensor(out, a, b, op).then_inc(o_ssm, 1)

            def state(start, end):
                for n in range(start, end):
                    j, n = divmod(n, O_SSM)
                    cos, sin = o_e[:, j % 2, 0], o_e[:, j % 2, 1]
                    b_re, b_im, x_re, x_im = ps[:, 2], ps[:, 3], full[:, 0], full[:, 1]
                    mag = o_mag[:, j:j + 1].to_broadcast([P, T])
                    if n == 0:
                        dve.wait_ge(o_bu, j + 1)
                        dve.wait_ge(o_e_done, 2 * j + 2)
                        op(j, o_a[:], cos, b_re, ALU.mult, 0)
                    if n == 1:
                        op(j, o_w[:], sin, b_im, ALU.mult, 0)
                    if n == 2:
                        op(j, o_a[:], o_a[:], o_w[:], ALU.add, 2)
                    if n == 3:
                        op(j, o_s[:], cos, b_im, ALU.mult, 0)
                    if n == 4:
                        op(j, o_w[:], sin, b_re, ALU.mult, 3)
                    if n == 5:
                        op(j, o_s[:], o_s[:], o_w[:], ALU.subtract, 5)
                    if n == 6:
                        nc.vector.tensor_tensor_scan(o_a[:], mag, o_a[:], 0.0, ALU.mult, ALU.add).then_inc(o_ssm, 1)
                    if n == 7:
                        dve.wait_ge(o_ssm, O_SSM * j + 6)
                        nc.vector.tensor_tensor_scan(o_s[:], mag, o_s[:], 0.0, ALU.mult, ALU.add).then_inc(o_ssm, 1)
                    if n == 8:
                        if j > 0:
                            dve.wait_ge(o_cy, j)
                        op(j, x_re, cos, o_a[:], ALU.mult, 7)
                    if n == 9:
                        op(j, o_w[:], sin, o_s[:], ALU.mult, 8)
                    if n == 10:
                        op(j, x_re, x_re, o_w[:], ALU.subtract, 10)
                    if n == 11:
                        op(j, x_im, cos, o_s[:], ALU.mult, 8)
                    if n == 12:
                        op(j, o_w[:], sin, o_a[:], ALU.mult, 11)
                    if n == 13:
                        op(j, x_im, x_im, o_w[:], ALU.add, 13)

            def inverse(n):
                dve.wait_ge(o_exp, n + 1)
                if n >= 2:
                    dve.wait_ge(o_scaled, n - 1)
                nc.vector.reciprocal(o_inv[n % 2], o_sum[n % 2]).then_inc(o_inverse, 1)

            at, step = 0, None
            for event, n in O_EVENTS:
                if event == "u":
                    split_low(dve, Unit(first + n + AHEAD))
                if event == "state":
                    state(at, at + 2)
                    if step is not None:
                        inverse(step)
                        step = None
                    state(at + 2, n)
                    at = n
                    dve.wait_ge(o_ssm, at)
                    if n == 8:
                        prepare_c()
                if event == "sum":
                    dve.wait_ge(o_roots, n + 1)
                    nc.vector.reciprocal(o_rstds2[n], o_roots2[n]).then_inc(o_rstds, 1)
                if event == "norm":
                    dve.wait_ge(o_lin, 5)

                    def latent_low(m):
                        dve.wait_ge(o_n_high, m + 1)
                        nc.vector.tensor_tensor(h_low[:, (2, 0, 1)[m]], o_lat[:, m], h_high[:, (2, 0, 1)[m]].bitcast(F32),
                                                ALU.subtract).then_inc(o_n_low, 1)

                    for m in range(3):
                        dve.wait_ge(o_spread, 1 if m == 0 else 2)
                        gain = par("kv_norm") if m == 0 else par("q_norm", m - 1)
                        nc.vector.scalar_tensor_tensor(out=o_lat[:, m], in0=o_lat[:, m], scalar=gain,
                                                       in1=ps[:, 6 if m > 0 else 5], op0=ALU.mult,
                                                       op1=ALU.mult).then_inc(o_normed, 1)
                        if m > 0:
                            latent_low(m - 1)
                    latent_low(2)
                    rope(0, ps[:, 7], o_kr)
                if event in ("kn", "v", "uq", "glu"):
                    split_low(dve, Unit(first + {"kn": O_KN, "v": O_VN, "uq": O_UQ, "glu": O_GLU}[event] + n + AHEAD))
                if event == "uq":
                    assert at % O_SSM in (0, 8)
                    rope(n + 1, ps[:, o_turn_bank(n)], o_q[:, n % 2, 2])
                if event == "step":
                    s, w, tr, v, end = o_step(n)
                    if step is not None:
                        inverse(step)
                    step = s
                    if s is not None:
                        width = (s % NBLK + 1) * P
                        bank = o_score_bank(s)
                        dve.wait_ge(o_scores, s + 1)
                        nc.vector.memset(ps[0:64, bank, width - 64:width], MASKED).then_inc(o_soft, 1)
                        dve.wait_ge(o_soft, O_SOFT * s + 1)
                        nc.vector.tensor_reduce(o_max, ps[:, bank, 0:width], AXIS.X, ALU.max).then_inc(o_soft, 1)
                        dve.wait_ge(o_soft, O_SOFT * s + 2)
                        if s >= 2:
                            dve.wait_ge(o_exp, s - 1)
                        nc.vector.tensor_scalar(o_neg[s % 2], o_max, -192 ** -0.5, None, op0=ALU.mult).then_inc(o_soft, 1)
                    if end is not None:
                        low(O_Y_HEAD[end], ps[:, o_pv_bank(end)])
                if event == "take":
                    dve.wait_ge(o_cy, 4 * n + 4)
                    nc.vector.scalar_tensor_tensor(out=o_us[:, n], in0=o_us[:, n], scalar=par("d_skip", n), in1=ps[:, 4],
                                                   op0=ALU.mult, op1=ALU.add).then_inc(o_taken, 1)
                if event == "gelu":
                    for m in range(2):
                        dve.wait_ge(o_z_high, m + 1)
                        nc.vector.tensor_tensor(h_low[:, 3 + m], o_us[:, m], h_high[:, 3 + m].bitcast(F32),
                                                ALU.subtract).then_inc(o_z_low, 1)
                if event == "gate":
                    for m in range(2):
                        dve.wait_ge(o_sig, m + 1)
                        dve.wait_ge(o_cy, SSM_TILES)
                        nc.vector.tensor_tensor(full[:, m], o_us[:, m], o_sg[:, m], ALU.mult).then_inc(o_gated, 1)
                    for m in range(2):
                        low(O_Y_SSM + m, full[:, m])
            out_take(dve, o, first + O_OUT, o_yacc, fresh=True, r=r, last=last)

        def o_gpsimd(pool):
            done = [0]

            def tt(out, a, b, op):
                nc.gpsimd.tensor_tensor(out, a, b, op).then_inc(o_small_done, 1)
                done[0] += 1
                pool.wait_ge(o_small_done, done[0])

            pool.wait_ge(o_prepared, 1)
            if "e" in names:
                pool.wait_ge(out_free, 8 * (O_NO["e"] + 1) + 2)
            early = o_e[:, 1].rearrange("p c (j n) -> p c j n", j=SSM_TILES)[:, :, :, 0:EB]
            for tab, size, power in ((early, EB, 0), (o_ea, EA, 5)):
                for c in range(2):
                    nc.gpsimd.memset(tab[:, c, :, 0:1], float(1 - c)).then_inc(o_small_done, 1)
                    done[0] += 1
                pool.wait_ge(o_small_done, done[0])
                n = 1
                while n < size:
                    shape = [P, SSM_TILES, n]
                    cos = o_cos[:, 8 * power:8 * power + 8].unsqueeze(2).to_broadcast(shape)
                    sin = o_sin[:, 8 * power:8 * power + 8].unsqueeze(2).to_broadcast(shape)
                    tmp = o_tmp[:, 0:SSM_TILES * n].rearrange("p (j n) -> p j n", j=SSM_TILES)
                    re, im = tab[:, 0, :, 0:n], tab[:, 1, :, 0:n]
                    new_re, new_im = tab[:, 0, :, n:2 * n], tab[:, 1, :, n:2 * n]
                    tt(new_re, re, cos, ALU.mult)
                    tt(tmp, im, sin, ALU.mult)
                    tt(new_re, new_re, tmp, ALU.subtract)
                    tt(new_im, im, cos, ALU.mult)
                    tt(tmp, re, sin, ALU.mult)
                    tt(new_im, new_im, tmp, ALU.add)
                    n, power = 2 * n, power + 1
            pool.wait_ge(rstd_spread, R_PRE["o"] + 1)
            nc.gpsimd.tensor_copy(o_eb, early).then_inc(o_small_done, 1)
            pool.wait_ge(o_small_done, done[0] + 1)
            done[0] += 1
            for j in range(SSM_TILES):
                shape = [P, EA, EB]
                a_cos, a_sin = (o_ea[:, c, j].unsqueeze(2).to_broadcast(shape) for c in range(2))
                b_cos_, b_sin_ = (o_eb[:, c, j].unsqueeze(1).to_broadcast(shape) for c in range(2))
                e_cos, e_sin = (o_e[:, j % 2, c].rearrange("p (a b) -> p a b", a=EA) for c in range(2))
                tmp = o_tmp.rearrange("p (a b) -> p a b", a=EA)
                if j >= 2:
                    pool.wait_ge(o_ssm, O_SSM * (j - 1))
                for out, first, second, op in ((e_cos, (a_cos, b_cos_), (a_sin, b_sin_), ALU.subtract),
                                               (e_sin, (a_sin, b_cos_), (a_cos, b_sin_), ALU.add)):
                    tt(out, first[0], first[1], ALU.mult)
                    tt(tmp, second[0], second[1], ALU.mult)
                    nc.gpsimd.tensor_tensor(out, out, tmp, op).then_inc(o_e_done, 1)
                    pool.wait_ge(o_e_done, 2 * j + (1 if op == ALU.subtract else 2))

        block = ctx.enter_context(nc.Block())

        @block.sync
        def _(sp):
            sp.dma_start(const[:], const_in).then_inc(const_loaded, 16)
            for s in range(RAW_SLOTS):
                sp.dma_start(raw[:, s], stream[s]).then_inc(weights_loaded[s], 16)
            with sp.Fori(1, total // RAW_SLOTS) as i:
                for s in range(RAW_SLOTS):
                    unit = stream[bass.ds(i * RAW_SLOTS + s, 1)].rearrange("a p n -> (a p) n")
                    sp.wait_ge(weights_low, i * RAW_SLOTS + (s + 1 - RAW_SLOTS))
                    sp.dma_start(raw[:, s], unit).then_inc(weights_loaded[s], 16)
            for k in range(KD):
                if names[-1] in P_NO:
                    sp.wait_ge(*post_done(P_NO[names[-1]], k))
                else:
                    sp.wait_ge(out_free, 8 * (O_NO[names[-1]] + OUTS[names[-1]]) - 5 + k)
                sp.dma_start(x_out[k * P:(k + 1) * P], x[:, k]).then_inc(x_stored, 16)
            sp.wait_ge(x_stored, 16 * KD)

        @block.scalar
        def _(act):
            for k in range(KD):
                act.dma_start(x[:, k], x_in[k * P:(k + 1) * P]).then_inc(x_loaded[k], 16)
            act.dma_start(params[:], params_in).then_inc(params_loaded, 16)
            if TABLED:
                act.dma_start(table[:], tables_in[TABLE_OF[TABLED[0]]]).then_inc(table_loaded, 16)
            act.sem_inc(a_silu, 2)
            act.sem_inc(f_silu, 2)
            act.wait_ge(const_loaded, 16)
            for k in range(KD):
                act.wait_ge(x_loaded[k], 16)
                norm_square(act, 0, k, x[:, k])
                if k == 3:
                    split_high(act, Unit(0))
            norm_root(act, 0)
            split_high(act, Unit(1))
            for n, name in enumerate(names):
                last = n == len(names) - 1
                r = R_POST.get(name, None if last else R_PRE[name] + 1)
                normalise_high(act, H_NO[name])
                if n == 0:
                    for s in range(2, AHEAD):
                        split_high(act, Unit(s))
                if name in ("a0", "a1"):
                    a_scalar(act, AGAIN[name], H_NO[name], FIRST[name], O_NO[name], Y_BASE[name], r, last)
                if name == "b":
                    b_scalar(act, FIRST[name], O_NO[name], Y_BASE[name], r, last)
                if name == "c":
                    c_scalar(act, FIRST[name], O_NO[name], Y_BASE[name], r)
                if name == "e":
                    e_scalar(act, FIRST[name], O_NO[name], Y_BASE[name], r, last)
                if name == "o":
                    o_scalar(act, FIRST[name], O_NO[name], Y_BASE[name], r, last)
                if name in ("f0", "f1"):
                    f_scalar(act, AGAIN[name], FIRST[name], O_NO[name], Y_BASE[name], r, last)
                if name in TABLED[:-1]:
                    act.dma_start(table[:], tables_in[TABLE_OF[TABLED[TABLED.index(name) + 1]]]).then_inc(table_loaded, 16)
                if name in P_NO and not last:
                    post_scalar(act, r + 1, P_NO[name])

        @block.vector
        def _(dve):
            dve.sem_inc(out_free, 2)
            dve.sem_inc(a_vector, 2 * A_STEPS)
            dve.sem_inc(f_full, 2)
            split_low(dve, Unit(0))
            for k in range(KD):
                dve.wait_ge(x_loaded[k], 16)
            dve.wait_ge(params_loaded, 16)
            dve.wait_ge(const_loaded, 16)
            for n, name in enumerate(names):
                last = n == len(names) - 1
                gain = {"a0": ("norm", 0), "b": ("norm", 8), "c": ("norm", 16), "a1": ("norm", 24)}.get(name, (name + "_pre", 0))
                normalise(dve, R_PRE[name], H_NO[name], gain, classes=name == "b")
                if n == 0:
                    for s in range(2, AHEAD):
                        split_low(dve, Unit(s))
                if n == 0 and name != "a0" and "o" in names:
                    o_prepare(dve, 0)
                    o_prepare(dve, 1)
                r = R_POST.get(name, None if last else R_PRE[name] + 1)
                if name in ("a0", "a1"):
                    a_vector_part(dve, name, AGAIN[name], H_NO[name], FIRST[name], O_NO[name], Y_BASE[name], r, last)
                if name == "b":
                    b_vector(dve, FIRST[name], O_NO[name], Y_BASE[name], r, last)
                if name == "c":
                    c_vector(dve, FIRST[name], O_NO[name], Y_BASE[name])
                if name == "e":
                    e_vector(dve, FIRST[name], O_NO[name], Y_BASE[name], r, last)
                if name == "o":
                    o_vector(dve, FIRST[name], O_NO[name], Y_BASE[name], r, last)
                if name in ("f0", "f1"):
                    f_vector(dve, AGAIN[name], FIRST[name], O_NO[name], Y_BASE[name], r, last)
                if name in P_NO:
                    post_vector(dve, r, P_NO[name], SANDWICH[name], name + "_post")

        @block.tensor
        def _(pe):
            pe.wait_ge(const_loaded, 16)
            norm_sum(pe, 0)
            for n, name in enumerate(names):
                last = n == len(names) - 1
                r = R_POST.get(name, None if last else R_PRE[name] + 1)
                if name in ("a0", "a1"):
                    a_tensor(pe, AGAIN[name], H_NO[name], FIRST[name], O_NO[name], Y_BASE[name], r, last)
                if name == "b":
                    b_tensor(pe, H_NO[name], FIRST[name], O_NO[name], Y_BASE[name], r, last)
                if name == "c":
                    c_tensor(pe, H_NO[name], FIRST[name], O_NO[name], Y_BASE[name], r)
                if name == "e":
                    e_tensor(pe, H_NO[name], FIRST[name], O_NO[name], Y_BASE[name], r, last)
                if name == "o":
                    o_tensor(pe, H_NO[name], FIRST[name], O_NO[name], Y_BASE[name], r, last)
                if name in ("f0", "f1"):
                    f_tensor(pe, AGAIN[name], H_NO[name], FIRST[name], O_NO[name], Y_BASE[name], r, last)
                if name in P_NO and not last:
                    norm_sum(pe, r + 1)

        @block.gpsimd
        def _(pool):
            nc.gpsimd.memset(norm_zero, 0.0).then_inc(zero_done, 1)
            norm_gather(pool, 0)
            for n, name in enumerate(names):
                last = n == len(names) - 1
                r = R_POST.get(name, None if last else R_PRE[name] + 1)
                if name == "b":
                    b_gpsimd(pool)
                if name == "e":
                    e_gpsimd(pool)
                if name == "o":
                    o_gpsimd(pool)
                if r is not None:
                    norm_gather(pool, r)
                if name in P_NO:
                    post_gpsimd(pool, P_NO[name])


def stream_b(w_in, w_out):
    units = []
    for half in range(2):
        for g in range(B_PATTERNS):
            units += [unit_wide(w_in, 2 * kk, (2 * B_PATTERNS + g) * D + half * T) for kk in range(4)]
        heads = range(4 * half, 4 * half + 4)
        for h in heads:
            for part in (1, 0):
                units += [unit_rows(w_in, (part * B_PATTERNS + g) * B_HEADS + h) for g in range(B_PATTERNS)]
        units += [unit_rows(w_in, 3 * B_PATTERNS * B_HEADS + h) for h in heads]
    return units + [unit_rows(w_out, m) for m in range(KD)]


def stream_c(w_in, w_grp, w_out):
    def xs(g):
        return [unit_rows(w_in, 4 * g + m) for m in range(4)]

    units = xs(0)
    for g in range(C_POOLS):
        units += [unit_rows(w_in, 16 + 4 * g + m) for m in range(4)]
        units += [unit_wide(w_grp[g], 0, 256 * n, 256) for n in range(2)]
        if g + 1 < C_POOLS:
            units += xs(g + 1)
        units += [unit_wide(w_out, 4 * g, 256 * n, 256) for n in range(4)]
    return units


def stream_e(w_in, w_out):
    def conv(m):
        return [unit_rows(w_in, 12 + m), unit_rows(w_in, 16 + m)]

    def head(h):
        return [unit_rows(w_in, h), unit_rows(w_in, 4 + h)]

    units = conv(0) + conv(1) + [unit_wide(w_in, 2 * kk, D) for kk in range(4)] + head(0) + head(1) + conv(2)
    units += head(2) + head(3) + conv(3)
    return units + [unit_rows(w_out, m) for m in range(KD)]


def stream_f(w_gate, w_up, w_down):
    units, start = [], 0
    for n in FF_GROUPS:
        for m in range(start, start + n):
            units += [unit_rows(w_gate, m), unit_rows(w_up, m)]
        units += [unit_rows(w_down[start * P:(start + n) * P], m) for m in range(KD)]
        start += n
    return units


def stream_o(w_in, w_uq, w_ukv, w_glu, w_out):
    u, cq, ckv, kr = w_in[:, :256], w_in[:, 256:512], w_in[:, 512:640], w_in[:, 640:704]
    units = [unit_rows(u, 0), unit_rows(u, 1), unit_rows(ckv, 0), unit_rows(cq, 0), unit_rows(cq, 1),
             unit_rows(np.concatenate([kr, kr], axis=1), 0)]
    kv = w_ukv.reshape(P, MLA_HEADS, 2, P)
    for part in range(2):
        n = np.zeros((P, UNIT), np.float32)
        n[:, :MLA_HEADS * P] = kv[:, :, part].reshape(P, -1)
        units.append(n)
    q = w_uq.reshape(2, P, MLA_HEADS, 192)
    for g in range(MLA_HEADS // 2):
        n = np.zeros((P, 2, T), np.float32)
        for k in range(2):
            n[:, k, :2 * P] = q[k, :, 2 * g:2 * g + 2, :P].reshape(P, -1)
            n[:, k, 2 * P:3 * P] = q[k, :, 2 * g:2 * g + 2, P:].reshape(P, -1)
        units.append(n.reshape(P, UNIT))
    glu = np.zeros((P, UNIT), np.float32)
    glu[:, :512] = w_glu.reshape(2, P, 256).transpose(1, 0, 2).reshape(P, 512)
    units.append(glu)
    rows = np.concatenate([w_out[256:], w_out[:256]])
    return units + [unit_rows(rows, m) for m in range(KD)]




def unit_rows(w, m):
    k = w.shape[0] // P
    u = np.zeros((P, UNIT), np.float32)
    u[:, :k * P] = w[:, m * P:(m + 1) * P].reshape(k, P, P).transpose(1, 0, 2).reshape(P, k * P)
    return u


def unit_wide(w, k0, c0, cols=T):
    n = UNIT // cols
    return w[k0 * P:(k0 + n) * P, c0:c0 + cols].reshape(n, P, cols).transpose(1, 0, 2).reshape(P, UNIT)


def stream_a(w_in, w_out):
    wu, wv, wz = w_in[:, :A_WIDTH], w_in[:, A_WIDTH:2 * A_WIDTH], w_in[:, 2 * A_WIDTH:]
    units = [unit_wide(wv, 2 * kk, T * c) for c in range(4) for kk in range(4)]
    for half in range(2):
        for m in range(8 * half, 8 * half + 8):
            units += [unit_rows(wu, m), unit_rows(wz, m)]
        units += [unit_rows(w_out[half * D:(half + 1) * D], m) for m in range(KD)]
    return units


def columns(v):
    return np.asarray(v).reshape(-1, P).T


def rotary_table(half, block, theta, order=None):
    inv = np.power(np.float32(theta), -np.arange(half, dtype=np.float32) / half).astype(np.float32)
    angle = np.arange(T, dtype=np.float32)[:, None] * inv[None, :]
    if order is not None:
        angle = angle[order]
    out = np.zeros((P, 2, T), np.float32)
    out[:, 0] = 1.0
    for b in range(0, P, block):
        for h in range(2):
            rows = slice(b + h * half, b + (h + 1) * half)
            out[rows, 0], out[rows, 1] = np.cos(angle).T, np.sin(angle).T
    return out.reshape(P, 2 * T)


def rotation(half, block):
    m = np.zeros((P, P), np.float32)
    for b in range(0, P, block):
        for i in range(half):
            m[b + i + half, b + i] = -1.0
            m[b + i, b + i + half] = 1.0
    return m


def class_masks():
    d = np.arange(P)[:, None] - np.arange(P)[None, :]
    blocks = [(d >= 0) & (d <= 31)] * 3 + [(d >= 0) & (d <= 32)] + [(d >= 1) & (d <= 32)] * 3
    blocks += [d >= 0, (d >= 0) & (d % 4 == 0)]
    return np.where(np.concatenate(blocks, axis=1), 0.0, MASKED).astype(np.float32)


def constants():
    c = np.zeros((P, N_CONST), np.float32)

    def put(name, v):
        c[:, CONST[name]:CONST[name] + v.shape[1]] = v

    put("ident", np.eye(P, dtype=np.float32))
    put("ones", np.ones((P, P), np.float32))
    put("causal", np.triu(np.ones((P, P), np.float32)))
    chunk = np.zeros((P, T), np.float32)
    chunk[:64, T - 64:] = MASKED
    put("chunk", chunk)
    put("rot_b", rotation(16, P))
    put("rot_e", rotation(8, 64))
    put("rot_o", rotation(32, 64))
    for g, w in enumerate(POOL_SIZES):
        n = np.minimum(np.arange(16) + 1, w).astype(np.float32)
        c[:, CONST["inv_count"] + 16 * g:CONST["inv_count"] + 16 * (g + 1)] = np.float32(1.0) / n
    c[:, CONST["eps"]] = EPS
    c[:, CONST["ln_eps"]] = LN_EPS
    return c


def lay_out(v):
    v = {k: np.asarray(a) for k, a in v.items()}
    streams = {
        "a0": lambda: stream_a(v["a_w_in"][0], v["a_w_out"][0]),
        "b": lambda: stream_b(v["b_w_in"][0], v["b_w_out"][0]),
        "c": lambda: stream_c(v["c_w_in"][0], v["c_w_grp"][0], v["c_w_out"][0]),
        "a1": lambda: stream_a(v["a_w_in"][1], v["a_w_out"][1]),
        "e": lambda: stream_e(v["l0_w_in_2"], v["l0_w_out_2"]),
        "f0": lambda: stream_f(v["l0_w_gate_2"], v["l0_w_up_2"], v["l0_w_down_2"]),
        "o": lambda: stream_o(v["l1_w_in_2"], v["l1_w_uq_2"], v["l1_w_ukv_2"], v["l1_w_glu_2"], v["l1_w_out_2"]),
        "f1": lambda: stream_f(v["l1_w_gate_2"], v["l1_w_up_2"], v["l1_w_down_2"])}
    units = [u for name in NAMES for u in streams[name]()]
    assert len(units) == TOTAL, (len(units), TOTAL)

    params = np.zeros((P, N_COLUMNS), np.float32)

    def put(name, a):
        params[:, COLUMNS[name]:COLUMNS[name] + a.shape[1]] = a

    for name, source in (("norm", "norm_gain"), ("e_pre", "l0_mix_pre_2"), ("e_post", "l0_mix_post_2"),
                         ("f0_pre", "l0_ffn_pre_2"), ("f0_post", "l0_ffn_post_2"), ("o_pre", "l1_mix_pre_2"),
                         ("o_post", "l1_mix_post_2"), ("f1_pre", "l1_ffn_pre_2"), ("f1_post", "l1_ffn_post_2"),
                         ("a_v", "a_v_gain"), ("b_q", "b_q_gain"), ("b_k", "b_k_gain"), ("c_scale", "c_scale"),
                         ("subln", "l0_subln_2"), ("dw_b", "l0_dw_b_2"), ("ln_g", "l0_conv_ln_g_2"),
                         ("ln_b", "l0_conv_ln_b_2"), ("glu_b", "l1_b_glu_2"), ("q_norm", "l1_q_norm_2"),
                         ("kv_norm", "l1_kv_norm_2"), ("a_re", "l1_a_re_2"), ("a_im", "l1_a_im_2"),
                         ("d_skip", "l1_d_skip_2")):
        put(name, columns(v[source]))
    put("dw_w", v["l0_dw_w_2"].reshape(CONV_WIDTH, CONV_TILES, P).transpose(2, 1, 0).reshape(P, -1))
    put("log_dt", columns(np.repeat(v["l1_log_dt_2"], 64)))
    rows = [v[f"l0_lambda_{n}_2"] for n in ("q1", "k1", "q2", "k2")]
    put("lambda", np.broadcast_to(np.concatenate(rows)[None], (P, 4 * DIFF_DIM)))

    tables = np.zeros((5, P, 2176), np.float32)
    for j, at in ((0, 0), (1, 2)):
        tables[at, :, :1024] = v["a_w_s"][j].transpose(2, 0, 1).reshape(P, 1024)
        tables[at, :, 1024:2048] = np.broadcast_to(v["a_b_s"][j].reshape(1, 1024), (P, 1024))
    by_class = np.arange(T).reshape(P, CLASSES).T.reshape(-1)
    tables[1, :, :2 * T] = rotary_table(16, P, 500000.0, by_class)
    tables[1, :, 2 * T:] = class_masks()
    tables[3, :, :2 * T] = rotary_table(8, 64, 500000.0)
    tables[4, :, :2 * T] = rotary_table(32, 64, 10000.0)

    b_mat, c_mat = np.zeros((P, 2, 2, P), np.float32), np.zeros((P, 2, SSM_TILES, 32), np.float32)
    for g in range(16):
        j, s, c = g // 2, (g % 2) * 64, (g % 2) * 16
        for part, (bn, cn) in enumerate((("l1_b_re_2", "l1_c_re_2"), ("l1_b_im_2", "l1_c_im_2"))):
            at = 32 * (j % 4) + c
            b_mat[at:at + 16, j // 4, part, s:s + 64] = v[bn][g].T
            c_mat[s:s + 64, part, j, c:c + 16] = v[cn][g].T
    ssm = np.concatenate([b_mat.reshape(P, -1), c_mat.reshape(P, -1)], axis=1)
    return {"stream": np.stack(units), "x_in": np.ascontiguousarray(v["x"][0].T), "params_in": params,
            "const_in": constants(), "tables_in": tables, "ssm_in": ssm}


def kernel(**inputs):
    import concourse.bacc as bacc
    from concourse.bass_utils import run_bass_kernel_spmd

    arrays = lay_out(inputs)
    nc = bacc.Bacc("TRN2", target_bir_lowering=False, num_devices=1)
    args = [nc.dram_tensor(n, a.shape, F32, kind="ExternalInput").ap() for n, a in arrays.items()]
    out = nc.dram_tensor("x_out", (D, T), F32, kind="ExternalOutput").ap()
    build(nc, *args, out)
    result = run_bass_kernel_spmd(nc, [arrays], core_ids=[0])
    return np.ascontiguousarray(result.results[0]["x_out"].T)[None]
```
